# Optimizing a Trainium2 kernel written in Bass

```python
import math
import jax, jax.numpy as jnp
from jax import lax
import numpy as np

D_MODEL = 2048
BATCH = 1
SEQ = 256
DEPTH = 1

D_MIX = D_MODEL
DA_WIDTH = D_MIX // 2
DA_HEADS = 8
DA_V_DIM = DA_WIDTH // DA_HEADS
DA_HEAD_DIM = DA_V_DIM // 2
HG_WIDTH = D_MIX - DA_WIDTH
HG_HEADS = 8
HG_V_DIM = HG_WIDTH // HG_HEADS
HG_K_DIM = 128
HG_KEY_WIDTH = HG_HEADS * HG_K_DIM
HG_CHUNK = 64
SPLIT_SIZES = (DA_WIDTH, DA_WIDTH, DA_WIDTH, HG_KEY_WIDTH, HG_KEY_WIDTH, HG_WIDTH, HG_WIDTH)
D_IN = sum(SPLIT_SIZES)
Q_BLOCK = 128
NUM_BUCKETS = 32
MAX_DISTANCE = 128
N_MEM = 256
MEM_HEADS = 4
MEM_HEAD_DIM = D_MODEL // MEM_HEADS
D_FF = 5632
CONV_WIDTH = 3
EPS = 1e-6


def rmsnorm(x, w):
    xf = x.astype(jnp.float32)
    y = xf * lax.rsqrt(jnp.mean(xf * xf, axis=-1, keepdims=True) + EPS)
    return (y * w.astype(jnp.float32)).astype(x.dtype)

def t5_bucket(rel):
    n = jnp.maximum(rel, 0)
    max_exact = NUM_BUCKETS // 2
    nf = jnp.maximum(n, 1).astype(jnp.float32)
    large = max_exact + (jnp.log(nf / max_exact) / math.log(MAX_DISTANCE / max_exact)
                         * (NUM_BUCKETS - max_exact)).astype(jnp.int32)
    large = jnp.minimum(large, NUM_BUCKETS - 1)
    return jnp.where(n < max_exact, n, large)

def diff_attention(q, k, v, lam, bias_table):
    B, S = q.shape[0], q.shape[1]
    nb = S // Q_BLOCK
    scale = DA_HEAD_DIM ** -0.5
    qb = q.reshape(B, nb, Q_BLOCK, DA_HEADS, 2, DA_HEAD_DIM).transpose(1, 0, 3, 4, 2, 5)
    kt = k.transpose(0, 2, 3, 1, 4)
    vt = v.transpose(0, 2, 1, 3)
    kpos = jnp.arange(S)

    def block(args):
        i, qi = args
        qpos = i * Q_BLOCK + jnp.arange(Q_BLOCK)
        rel = qpos[:, None] - kpos[None, :]
        bias = bias_table[t5_bucket(rel)].transpose(2, 0, 1).astype(jnp.float32)
        logits = jnp.einsum('bhmqd,bhmkd->bhmqk', qi, kt).astype(jnp.float32) * scale
        logits = logits + bias[None, :, None]
        logits = jnp.where(rel >= 0, logits, -1e30)
        p = jax.nn.softmax(logits, axis=-1)
        a = p[:, :, 0] - lam * p[:, :, 1]
        return jnp.einsum('bhqk,bhkv->bhqv', a.astype(v.dtype), vt)

    out = lax.map(block, (jnp.arange(nb), qb))
    return out.transpose(1, 0, 3, 2, 4).reshape(B, S, DA_HEADS, DA_V_DIM)

def hgrn2(q, fz, i, lb):
    B, S = q.shape[0], q.shape[1]
    nc = S // HG_CHUNK
    f32 = jnp.float32
    f = lb + (1.0 - lb) * jax.nn.sigmoid(fz.astype(f32))
    log_f = jnp.log(f)
    kk = 1.0 - f

    def to_chunks(t):
        return t.astype(f32).reshape(B, nc, HG_CHUNK, HG_HEADS, t.shape[-1]).transpose(1, 0, 3, 2, 4)

    qc, kc, vc, gc = to_chunks(q), to_chunks(kk), to_chunks(i), to_chunks(log_f)
    causal = jnp.tril(jnp.ones((HG_CHUNK, HG_CHUNK), dtype=bool))[:, :, None]

    def step(state, inp):
        q_c, k_c, v_c, g_c = inp
        G = jnp.cumsum(g_c, axis=2)
        o_inter = jnp.einsum('bhck,bhkv->bhcv', q_c * jnp.exp(G), state)
        diff = G[:, :, :, None, :] - G[:, :, None, :, :]
        decay = jnp.where(causal, jnp.exp(jnp.where(causal, diff, 0.0)), 0.0)
        a = jnp.einsum('bhtk,bhsk,bhtsk->bhts', q_c, k_c, decay)
        o_intra = jnp.einsum('bhts,bhsv->bhtv', a, v_c)
        g_last = G[:, :, -1]
        k_dec = k_c * jnp.exp(g_last[:, :, None, :] - G)
        new_state = jnp.exp(g_last)[..., None] * state + jnp.einsum('bhsk,bhsv->bhkv', k_dec, v_c)
        return new_state, o_inter + o_intra

    s0 = jnp.zeros((B, HG_HEADS, HG_K_DIM, HG_V_DIM), f32)
    _, o = lax.scan(step, s0, (qc, kc, vc, gc))
    return o.transpose(1, 0, 3, 2, 4).reshape(B, S, HG_HEADS, HG_V_DIM).astype(i.dtype)

def causal_dwconv(u, w, b):
    S = u.shape[1]
    up = jnp.pad(u, ((0, 0), (CONV_WIDTH - 1, 0), (0, 0)))
    return sum(w[j] * up[:, j:j + S] for j in range(CONV_WIDTH)) + b

def split_points():
    pts, acc = [], 0
    for s in SPLIT_SIZES[:-1]:
        acc += s
        pts.append(acc)
    return pts

def first_inputs(seed: int = 0) -> dict:
    key = jax.random.key(seed)
    ks = jax.random.split(key, 24)
    f32 = jnp.float32

    def nrm(k, shape, scale):
        return jax.random.normal(k, shape, f32) * scale

    def gain(k, shape):
        return 1.0 + 0.1 * jax.random.normal(k, shape, f32)

    L = DEPTH
    return {
        "x": nrm(ks[0], (BATCH, SEQ, D_MODEL), 1.0),
        "mem": nrm(ks[1], (BATCH, N_MEM, D_MODEL), 1.0),
        "w_in": nrm(ks[2], (L, D_MODEL, D_IN), D_MODEL ** -0.5),
        "w_out": nrm(ks[3], (L, D_MIX, D_MODEL), D_MIX ** -0.5),
        "norm_mix_w": gain(ks[4], (L, D_MODEL)),
        "lam_q1": nrm(ks[5], (L, DA_HEAD_DIM), 0.1),
        "lam_k1": nrm(ks[6], (L, DA_HEAD_DIM), 0.1),
        "lam_q2": nrm(ks[7], (L, DA_HEAD_DIM), 0.1),
        "lam_k2": nrm(ks[8], (L, DA_HEAD_DIM), 0.1),
        "da_subln_w": gain(ks[9], (L, DA_V_DIM)),
        "hg_lb_raw": nrm(ks[10], (L + 1, HG_KEY_WIDTH), 0.5),
        "hg_norm_w": gain(ks[11], (L, HG_V_DIM)),
        "rel_bias": nrm(ks[12], (NUM_BUCKETS, DA_HEADS), 0.5),
        "norm_mem_w": gain(ks[13], (L, D_MODEL)),
        "mem_kv_norm_w": gain(ks[14], (L, D_MODEL)),
        "w_mq": nrm(ks[15], (L, D_MODEL, D_MODEL), D_MODEL ** -0.5),
        "w_mkv": nrm(ks[16], (L, D_MODEL, 2 * D_MODEL), D_MODEL ** -0.5),
        "w_mo": nrm(ks[17], (L, D_MODEL, D_MODEL), D_MODEL ** -0.5),
        "norm_ffn_w": gain(ks[18], (L, D_MODEL)),
        "w_up": nrm(ks[19], (L, D_MODEL, 2 * D_FF), D_MODEL ** -0.5),
        "conv_w": nrm(ks[20], (L, CONV_WIDTH, 2 * D_FF), CONV_WIDTH ** -0.5),
        "conv_b": nrm(ks[21], (L, 2 * D_FF), 0.02),
        "w_down": nrm(ks[22], (L, D_FF, D_MODEL), D_FF ** -0.5),
        "final_norm_w": gain(ks[23], (D_MODEL,)),
    }

def first_block(x, mem, w_in, w_out, norm_mix_w, lam_q1, lam_k1, lam_q2, lam_k2, da_subln_w,
              hg_lb_raw, hg_norm_w, rel_bias, norm_mem_w, mem_kv_norm_w, w_mq, w_mkv, w_mo,
              norm_ffn_w, w_up, conv_w, conv_b, w_down, final_norm_w):
    B, S, _ = x.shape
    f32 = jnp.float32
    lb_all = jnp.cumsum(jax.nn.softmax(hg_lb_raw.astype(f32), axis=0), axis=0)
    pts = split_points()
    for layer in range(DEPTH):
        h = rmsnorm(x, norm_mix_w[layer])
        proj = h @ w_in[layer]
        da_q, da_k, da_v, hg_q, hg_f, hg_i, hg_g = jnp.split(proj, pts, axis=-1)

        lam_init = 0.8 - 0.6 * math.exp(-0.3 * layer)
        lam = (jnp.exp(jnp.sum(lam_q1[layer].astype(f32) * lam_k1[layer].astype(f32)))
               - jnp.exp(jnp.sum(lam_q2[layer].astype(f32) * lam_k2[layer].astype(f32)))
               + lam_init)
        da_o = diff_attention(da_q.reshape(B, S, DA_HEADS, 2, DA_HEAD_DIM),
                              da_k.reshape(B, S, DA_HEADS, 2, DA_HEAD_DIM),
                              da_v.reshape(B, S, DA_HEADS, DA_V_DIM), lam, rel_bias)
        da_o = rmsnorm(da_o, da_subln_w[layer]) * (1.0 - lam_init)

        lb = lb_all[layer].reshape(HG_HEADS, HG_K_DIM)
        hg_o = hgrn2(hg_q.reshape(B, S, HG_HEADS, HG_K_DIM),
                     hg_f.reshape(B, S, HG_HEADS, HG_K_DIM),
                     hg_i.reshape(B, S, HG_HEADS, HG_V_DIM), lb)
        hg_o = rmsnorm(hg_o, hg_norm_w[layer]) * jax.nn.silu(hg_g.reshape(B, S, HG_HEADS, HG_V_DIM))

        mix = jnp.concatenate([da_o.reshape(B, S, DA_WIDTH), hg_o.reshape(B, S, HG_WIDTH)], axis=-1)
        x = x + mix @ w_out[layer]

        hq = rmsnorm(x, norm_mem_w[layer])
        mk = rmsnorm(mem, mem_kv_norm_w[layer])
        mq = (hq @ w_mq[layer]).reshape(B, S, MEM_HEADS, MEM_HEAD_DIM)
        m_k, m_v = jnp.split(mk @ w_mkv[layer], 2, axis=-1)
        m_k = m_k.reshape(B, N_MEM, MEM_HEADS, MEM_HEAD_DIM)
        m_v = m_v.reshape(B, N_MEM, MEM_HEADS, MEM_HEAD_DIM)
        m_logits = jnp.einsum('bqhd,bkhd->bhqk', mq, m_k).astype(f32) * (MEM_HEAD_DIM ** -0.5)
        m_p = jax.nn.softmax(m_logits, axis=-1).astype(x.dtype)
        m_o = jnp.einsum('bhqk,bkhd->bqhd', m_p, m_v).reshape(B, S, D_MODEL)
        x = x + m_o @ w_mo[layer]

        hf = rmsnorm(x, norm_ffn_w[layer])
        u = causal_dwconv(hf @ w_up[layer], conv_w[layer], conv_b[layer])
        a, b = jnp.split(u, 2, axis=-1)
        x = x + (jax.nn.silu(a) * b) @ w_down[layer]
    return rmsnorm(x, final_norm_w)


CHUNK = 64
HEAD_DIM = 128
D_MIX_2 = D_MODEL
W_A = 6 * HEAD_DIM
W_B = 6 * HEAD_DIM
N_POOL_GROUPS = 4
POOL_WINDOWS = (2, 4, 8, 16)
G_C = HEAD_DIM
W_C = N_POOL_GROUPS * G_C
D_IN_TOT = 3 * W_A + 2 * W_B + W_C
K_SHORT = 3
K_CONFORMER = 31
K_FFN = 3
RMS_EPS = 1e-6
LN_EPS = 1e-5


def rms_norm(x, g):
    xf = x.astype(jnp.float32)
    y = xf * lax.rsqrt(jnp.mean(xf * xf, axis=-1, keepdims=True) + RMS_EPS)
    return (y * g.astype(jnp.float32)).astype(x.dtype)

def layer_norm(x, g, b):
    xf = x.astype(jnp.float32)
    mu = jnp.mean(xf, axis=-1, keepdims=True)
    var = jnp.mean(jnp.square(xf - mu), axis=-1, keepdims=True)
    y = (xf - mu) * lax.rsqrt(var + LN_EPS)
    return (y * g.astype(jnp.float32) + b.astype(jnp.float32)).astype(x.dtype)

def causal_depthwise_conv(x, w):
    k, c = w.shape
    return lax.conv_general_dilated(
        x, w[:, None, :].astype(x.dtype),
        window_strides=(1,), padding=[(k - 1, 0)],
        dimension_numbers=("NWC", "WIO", "NWC"),
        feature_group_count=c)

def trailing_mean_minus_self(x, window):
    s = x.shape[1]
    xf = x.astype(jnp.float32)
    c = jnp.cumsum(xf, axis=1)
    c_shift = jnp.pad(c, ((0, 0), (window, 0), (0, 0)))[:, :s]
    counts = jnp.minimum(jnp.arange(1, s + 1, dtype=jnp.float32), float(window))[None, :, None]
    return ((c - c_shift) / counts - xf).astype(x.dtype)

def short_gated_conv_mixer(u_a, conv_w):
    b_gate, c_gate, v = jnp.split(u_a, 3, axis=-1)
    return b_gate * causal_depthwise_conv(c_gate * v, conv_w)

def conformer_conv_mixer(u_b, conv_w, conv_b, ln_g, ln_b):
    val, gate = jnp.split(u_b, 2, axis=-1)
    glu = val * jax.nn.sigmoid(gate)
    y = causal_depthwise_conv(glu, conv_w) + conv_b
    y = layer_norm(y, ln_g, ln_b)
    return jax.nn.silu(y)

def multiscale_pool_mixer(u_c, pool_w, pool_scale):
    bsz, s, _ = u_c.shape
    groups = u_c.reshape(bsz, s, N_POOL_GROUPS, G_C)
    pooled = jnp.stack(
        [trailing_mean_minus_self(groups[:, :, gi], w) for gi, w in enumerate(POOL_WINDOWS)],
        axis=2)
    mixed = jnp.einsum("bsgc,gcd->bsgd", pooled, pool_w)
    return mixed.reshape(bsz, s, W_C) * pool_scale

def conv_gated_mlp(h, w_up, conv_w, conv_b, w_down):
    up = h @ w_up
    up = causal_depthwise_conv(up, conv_w) + conv_b
    gate, val = jnp.split(up, 2, axis=-1)
    return (jax.nn.silu(gate) * val) @ w_down

def second_inputs(seed: int = 0) -> dict:
    key = jax.random.key(seed)
    ks = jax.random.split(key, 20)
    f32 = jnp.float32
    nrm = lambda k, shape, scale: jax.random.normal(k, shape, f32) * scale
    gain = lambda k, shape: 1.0 + 0.05 * jax.random.normal(k, shape, f32)
    return {
        "x": jax.random.normal(ks[0], (BATCH, SEQ, D_MODEL), f32),
        "norm_mix_pre": gain(ks[1], (DEPTH, D_MODEL)),
        "norm_mix_post": gain(ks[2], (DEPTH, D_MODEL)),
        "norm_ffn_pre": gain(ks[3], (DEPTH, D_MODEL)),
        "norm_ffn_post": gain(ks[4], (DEPTH, D_MODEL)),
        "w_in": nrm(ks[5], (DEPTH, D_MODEL, D_IN_TOT), D_MODEL ** -0.5),
        "conv_a_w": nrm(ks[6], (DEPTH, K_SHORT, W_A), K_SHORT ** -0.5),
        "conv_b_w": nrm(ks[7], (DEPTH, K_CONFORMER, W_B), K_CONFORMER ** -0.5),
        "conv_b_bias": nrm(ks[8], (DEPTH, W_B), 0.01),
        "ln_b_gain": gain(ks[9], (DEPTH, W_B)),
        "ln_b_bias": nrm(ks[10], (DEPTH, W_B), 0.01),
        "pool_w": nrm(ks[11], (DEPTH, N_POOL_GROUPS, G_C, G_C), G_C ** -0.5),
        "pool_scale": 1.0 + 0.1 * jax.random.normal(ks[12], (DEPTH, W_C), f32),
        "w_out": nrm(ks[13], (DEPTH, D_MIX_2, D_MODEL), D_MIX_2 ** -0.5),
        "w_up": nrm(ks[14], (DEPTH, D_MODEL, 2 * D_FF), D_MODEL ** -0.5),
        "conv_ffn_w": nrm(ks[15], (DEPTH, K_FFN, 2 * D_FF), K_FFN ** -0.5),
        "conv_ffn_bias": nrm(ks[16], (DEPTH, 2 * D_FF), 0.01),
        "w_down": nrm(ks[17], (DEPTH, D_FF, D_MODEL), D_FF ** -0.5),
    }

def second_block(x, norm_mix_pre, norm_mix_post, norm_ffn_pre, norm_ffn_post,
              w_in, conv_a_w, conv_b_w, conv_b_bias, ln_b_gain, ln_b_bias,
              pool_w, pool_scale, w_out, w_up, conv_ffn_w, conv_ffn_bias, w_down):
    for l in range(DEPTH):
        h = rms_norm(x, norm_mix_pre[l])
        u = h @ w_in[l]
        u_a = u[..., :3 * W_A]
        u_b = u[..., 3 * W_A:3 * W_A + 2 * W_B]
        u_c = u[..., 3 * W_A + 2 * W_B:]
        y_a = short_gated_conv_mixer(u_a, conv_a_w[l])
        y_b = conformer_conv_mixer(u_b, conv_b_w[l], conv_b_bias[l], ln_b_gain[l], ln_b_bias[l])
        y_c = multiscale_pool_mixer(u_c, pool_w[l], pool_scale[l])
        y = jnp.concatenate([y_a, y_b, y_c], axis=-1) @ w_out[l]
        x = x + rms_norm(y, norm_mix_post[l])
        h = rms_norm(x, norm_ffn_pre[l])
        f = conv_gated_mlp(h, w_up[l], conv_ffn_w[l], conv_ffn_bias[l], w_down[l])
        x = x + rms_norm(f, norm_ffn_post[l])
    return x


def setup_inputs(seed=0):
    out = dict(first_inputs(seed))
    for name, value in second_inputs(seed + 1).items():
        if name != "x":
            out[name + "_2"] = value
    return out


def reference(
    x, mem, w_in, w_out, norm_mix_w, lam_q1, lam_k1, lam_q2, lam_k2, da_subln_w, hg_lb_raw,
    hg_norm_w, rel_bias, norm_mem_w, mem_kv_norm_w, w_mq, w_mkv, w_mo, norm_ffn_w, w_up, conv_w,
    conv_b, w_down, final_norm_w, norm_mix_pre_2, norm_mix_post_2, norm_ffn_pre_2,
    norm_ffn_post_2, w_in_2, conv_a_w_2, conv_b_w_2, conv_b_bias_2, ln_b_gain_2, ln_b_bias_2,
    pool_w_2, pool_scale_2, w_out_2, w_up_2, conv_ffn_w_2, conv_ffn_bias_2, w_down_2,
):
    x = first_block(
        x, mem, w_in, w_out, norm_mix_w, lam_q1, lam_k1, lam_q2, lam_k2, da_subln_w, hg_lb_raw,
        hg_norm_w, rel_bias, norm_mem_w, mem_kv_norm_w, w_mq, w_mkv, w_mo, norm_ffn_w, w_up,
        conv_w, conv_b, w_down, final_norm_w,
    )
    return second_block(
        x, norm_mix_pre_2, norm_mix_post_2, norm_ffn_pre_2, norm_ffn_post_2, w_in_2, conv_a_w_2,
        conv_b_w_2, conv_b_bias_2, ln_b_gain_2, ln_b_bias_2, pool_w_2, pool_scale_2, w_out_2,
        w_up_2, conv_ffn_w_2, conv_ffn_bias_2, w_down_2,
    )


_drawn_inputs = setup_inputs


def setup_inputs(seed=0):
    import zlib

    import numpy as np

    out = dict(_drawn_inputs(seed))
    spreads = {}
    factors = {'lam_q1': 8.0,
     'norm_mem_w': 4.077,
     'mem_kv_norm_w': 2.868,
     'conv_b': 3.121,
     'conv_b_bias_2': 6.047,
     'ln_b_bias_2': 8.0,
     'conv_ffn_bias_2': 7.009}
    for name, (base, spread) in spreads.items():
        noise = np.random.default_rng([zlib.crc32(name.encode()), seed]).standard_normal(out[name].shape)
        drawn = base * np.exp(spread * noise) if base else spread * noise
        out[name] = __import__('jax').numpy.asarray(drawn.astype(out[name].dtype))
    for name, factor in factors.items():
        out[name] = (out[name] * factor).astype(out[name].dtype)
    return out
```

```python
import concourse.bass as bass
from concourse import mybir
from contextlib import ExitStack, contextmanager

F32 = mybir.dt.float32
F32R = mybir.dt.float32r
U32 = mybir.dt.uint32
ALU = mybir.AluOpType
ACT = mybir.ActivationFunctionType
AX = mybir.AxisListType.X

P = 128
TOK = 256
DM = 2048
KT = DM // P
FF = 5632
FT = FF // P
HEADS = 8
CH = 64
NCHK = TOK // CH
MH = 4
MHT = KT // MH
CONF_TAPS = 31
WB = 768
SLOTS = 4
CW = 1024
BANK = 512
EPS = 1e-6
LN_EPS = 1e-5
NEG = -1e30
BIAS_SCALE = 8.0
LAM_INIT = 0.2
WINDOWS = (2, 4, 8, 16)
NREL = 384
UPAD = 2
PPAD = 16
GPAD = CONF_TAPS - 1

GEMMS = [
    ("da_fm", 8, 2, KT, False, "dve"), ("da_v", 8, 1, KT, True, "act"), ("hg_i", 8, 1, KT, True, "act"),
    ("hg_fm", 8, 3, KT, False, "dve"), ("out", 8, 2, KT, False, "x"), ("mem_k", 8, 2, KT, False, "dve"),
    ("mem_v", 8, 2, KT, True, "act"), ("mem_q", 8, 2, KT, False, "dve"), ("mem_o", 8, 2, KT, False, "x"),
    ("up", 8, 11, KT, False, "dve"), ("down", 8, 2, FT, False, "x"), ("conf", 4, 3, KT, False, "dve"),
    ("pool", 4, 1, KT, False, "dve"), ("gated", 6, 3, KT, False, "dve"), ("out_2", 8, 2, KT, False, "act"),
    ("up_2", 8, 11, KT, False, "dve"), ("down_2", 8, 2, FT, False, "act"),
]


class Gemm:
    pass


def plan():
    found, chunk, block = {}, 0, 0
    evac = {"act": 0, "dve": 0, "x": 0}
    for name, tiles, blocks, kt, token_major, reader in GEMMS:
        g = Gemm()
        g.name, g.tiles, g.blocks, g.kt, g.token_major, g.reader = name, tiles, blocks, kt, token_major, reader
        g.chunks = kt * tiles // 8
        g.first_chunk = chunk
        g.first_block = block
        g.banks = tiles // 2
        g.first_evac = evac[reader]
        g.before = found[GEMMS[len(found) - 1][0]] if found else None
        chunk += g.chunks * blocks
        block += blocks
        evac[reader] += g.banks * blocks
        g.end_chunk = chunk
        g.end_evac = evac[reader]
        found[name] = g
    return found, chunk


STATS = [("da_fm", 0), ("mem_k", 1), ("mem_q", 0), ("up", 1), ("conf", 0), ("up_2", 0), ("up_2", 1), ("down_2", 0)]
STD_END = [2, 4, 5, 6, 8, 9, 10, 11]


def sum_banks(gemms):
    return [3 + 4 * ((gemms[name].first_block + (n not in (5, 7))) % 2) for n, (name, _) in enumerate(STATS)]


GROUPS = [
    ("in", 8, False), ("mix_a", 4, True), ("mix_h", 4, True), ("mem", 8, False), ("mem_q", 8, False),
    ("mem_o", 8, False), ("up", 8, False), ("down", FT, True), ("in_2", 8, False),
    ("pool", 2, False), ("gated", 1, True), ("conf", 3, False), ("gated_on", 2, True), ("up_2", 8, False), ("down_2", FT, True),
]


def group_plan():
    ready, src, r, s = {}, {}, 0, 0
    for name, n, by_dve in GROUPS:
        ready[name], src[name] = r, s
        r += n
        s += n if by_dve else 0
    return ready, src


def gated_group(of, b):
    return of["gated"] if b == 0 else of["gated_on"] + b - 1


PARAMS = [
    ("norm_mix_w", KT), ("norm_mem_w", KT), ("mem_kv_norm_w", KT), ("norm_ffn_w", KT), ("final_norm_w", KT),
    ("norm_mix_pre_2", KT), ("norm_mix_post_2", KT), ("norm_ffn_pre_2", KT), ("norm_ffn_post_2", KT),
    ("conv_w", 3 * 2 * FT), ("conv_b", 2 * FT), ("conv_ffn_w_2", 3 * 2 * FT), ("conv_ffn_bias_2", 2 * FT),
    ("conv_a_w_2", 18), ("conv_b_w_2", 6 * CONF_TAPS), ("conv_b_bias_2", 6), ("ln_b_gain_2", 6),
    ("ln_b_bias_2", 6), ("pool_scale_2", 4), ("hg_lb_raw", 16), ("da_subln_w", 1), ("hg_norm_w", 1),
]
PCOL = {}
NPAR = 0
for _name, _n in PARAMS:
    PCOL[_name] = NPAR
    NPAR += _n

CONSTS = [
    ("ident", P), ("ones", P), ("inv_count", 4 * PPAD), ("eps", 2),
]
CCOL = {}
NCON = 0
for _name, _n in CONSTS:
    CCOL[_name] = NCON
    NCON += _n


def spread(ap, n):
    dims = [list(d) for d in ap.ap]
    return bass.AP(ap.tensor, ap.offset, [dims[0], [0, n]] + dims[1:])


def stretch(ap, n):
    dims = [list(d) for d in ap.ap]
    return bass.AP(ap.tensor, ap.offset, dims + [[0, n]])


LEVELS, CARRY, NHG = 0, 7 * P, 7 * P + TOK


class Steps:

    def __init__(self, eng, sem, count=0):
        self.eng, self.sem, self.n, self.off = eng, sem, count, 0

    def inc(self, ins):
        ins.then_inc(self.sem, 1)
        self.n += 1
        return self.n + self.off

    def wait(self, value=None):
        self.eng.wait_ge(self.sem, self.n + self.off if value is None else value)

    @contextmanager
    def loop(self, reg, passes, per):
        start = self.n
        self.off = reg * per
        yield
        assert self.n - start == per, (self.n - start, per)
        self.off = 0
        self.n = start + passes * per


def build(nc, A):
    GM, NCHUNK = plan()
    READY, SRC = group_plan()
    SUM_BANK = sum_banks(GM)
    ctx = ExitStack()
    with ctx:
        at = [16512]

        def place(name, shape, dt=F32, offset=None):
            size = 4
            for d in shape[1:]:
                size *= d
            where = at[0] if offset is None else offset
            if offset is None:
                at[0] += (size + 31) // 32 * 32
            return nc.alloc_sbuf_tensor_at(name, shape, dt, offset=where)

        def sem(name):
            return ctx.enter_context(nc.semaphore(name))

        raw = place("raw", [P, SLOTS, CW])
        w_hi = place("w_hi", [P, SLOTS, CW], F32R)
        w_lo = place("w_lo", [P, SLOTS, CW], F32R)
        x_at = at[0]
        x = place("x_res", [P, KT, TOK])
        op_at = at[0]
        op_hi = place("op_hi", [P, KT, TOK], F32R)
        op_lo = place("op_lo", [P, KT, TOK], F32R)
        par = place("par", [P, NPAR])
        con = place("con", [P, NCON])
        small = place("small", [P, 64])
        relb = place("relb", [P, HEADS])
        decay = place("decay", [P, HEADS, NCHK])
        w_pair = place("w_pair", [P, 2, KT])
        rstd = place("rstd", [P, 2, TOK])
        arena = at[0]
        end = 229344
        room = end - arena
        KB = 1024

        def inside(name, shape, offset, dt=F32):
            size = 4
            for d in shape[1:]:
                size *= d
            assert offset + size <= room, (name, offset, size, room)
            return place(name, shape, dt, offset=arena + offset)

        st = (room - 8 * KB) // 32 * 32
        sqb = inside("sqb", [P, 2, 2, TOK], st)
        sumsq = inside("sumsq", [P, 2, TOK], st + 4 * KB)
        sumsq_w = inside("sumsq_w", [P, 2, TOK], st + 6 * KB)
        hbuf = inside("hbuf", [P, 4, 2, TOK], 84 * KB)
        hg_con = inside("hg_con", [P, NHG], (room - 5 * KB) // 32 * 32)

        proj = inside("proj", [P, 40, TOK], 0)
        tokv = inside("tokv", [P, 2, 2, CW], 40 * KB)
        bias = inside("bias", [P, HEADS, TOK], 56 * KB)
        rel_rev = inside("rel_rev", [P, HEADS, TOK], 64 * KB)
        rel_row = inside("rel_row", [HEADS, NREL], 72 * KB)
        onehot = inside("onehot", [33, NREL], 74 * KB)
        flip = inside("flip", [P, P], 77 * KB)
        logit = inside("logit", [P, 2, 2, TOK], 64 * KB)
        attn = inside("attn", [P, 2, TOK], 68 * KB)
        attn_t = inside("attn_t", [P, 2, TOK], 70 * KB)
        da_o = inside("da_o", [P, HEADS, TOK], 72 * KB)
        da_sq = inside("da_sq", [P, HEADS, TOK], 24 * KB)
        da_rs = inside("da_rs", [P, HEADS, TOK], 32 * KB)
        lam_in = inside("lam_in", [P, 4, 64], 76 * KB)
        slab = lambda name, kb: inside(name, [P, HEADS, TOK], kb * KB)
        r_kk = slab("r_kk", 8)
        r_c, r_d, r_e, r_f = slab("r_c", 88), slab("r_d", 56), slab("r_e", 64), slab("r_f", 40)
        r_h, r_j = slab("r_h", 80), slab("r_j", 72)
        r_a = place("r_a", [P, HEADS, TOK], offset=x_at)
        r_b = place("r_b", [P, HEADS, TOK], offset=x_at + 8 * KB)
        state = inside("state", [P, 3, HEADS, P], 24 * KB)
        mem_x = inside("mem_x", [P, KT, TOK], 0)
        mq = inside("mq", [P, KT, TOK], 0)
        mk = inside("mk", [P, KT, TOK], 16 * KB)
        mv = inside("mv", [P, 2, DM], 32 * KB)
        mp = inside("mp", [P, 2, TOK], 48 * KB)
        mp_t = inside("mp_t", [P, 2, 2, TOK], 50 * KB)
        g_hi = inside("g_hi", [P, FT, TOK], 0, F32R)
        g_lo = inside("g_lo", [P, FT, TOK], FT * KB, F32R)
        up = inside("up_s", [P, 8, UPAD + TOK], 2 * FT * KB)
        cg = inside("cg", [P, 2, TOK], 2 * FT * KB + 32 * (UPAD + TOK))
        cv = inside("cv", [P, 2, TOK], 2 * FT * KB + 32 * (UPAD + TOK) + 2 * KB)
        y_hi = inside("y_hi", [P, KT, TOK], 0, F32R)
        y_lo = inside("y_lo", [P, KT, TOK], 16 * KB, F32R)
        glu = inside("glu", [P, 6, GPAD + TOK], 32 * KB)
        acc = inside("acc", [P, 6, TOK], 39 * KB)
        ub = inside("ub", [P, 2, 2, TOK], 45 * KB)
        ua = inside("ua", [P, 3, 2, TOK], 49 * KB)
        cvp = inside("cvp", [P, 2, UPAD + TOK], 55 * KB)
        ya = inside("ya", [P, 2, TOK], 58 * KB)
        px = inside("px", [P, 4, PPAD + TOK], 60 * KB)
        pa = inside("pa", [P, 4, PPAD + TOK], 65 * KB)
        pb = inside("pb", [P, 4, PPAD + TOK], 70 * KB)
        pw = inside("pw", [P, 4, P], 75 * KB)
        lnz = inside("lnz", [P, 6, TOK], 77 * KB)
        yres = place("yres", [P, KT, TOK], F32, offset=op_at)

        ps = ctx.enter_context(nc.psum_tensor("ps", [P, 8, BANK], F32))
        rel_dram = nc.dram_tensor("rel_dram", [HEADS, NREL], F32, kind="Internal").ap()

        def pc(name, i=0, n=1):
            return par[:, PCOL[name] + i:PCOL[name] + i + n]

        def cc(name, i=0, n=P):
            return con[:, CCOL[name] + i:CCOL[name] + i + n]

        ident, ones = cc("ident"), cc("ones")

        raw_loaded = [sem(f"raw_loaded{i}") for i in range(SLOTS)]
        params_loaded, consts_loaded, x_loaded = sem("params_loaded"), sem("consts_loaded"), sem("x_loaded")
        mem_loaded, pool_w_loaded = sem("mem_loaded"), sem("pool_w_loaded")
        table_loaded, rel_stored, rel_loaded = sem("table_loaded"), sem("rel_stored"), sem("rel_loaded")
        hi_rounded, chunk_split, chunk_used = sem("hi_rounded"), sem("chunk_split"), sem("chunk_used")
        act_evac, dve_evac, x_updated = sem("act_evac"), sem("dve_evac"), sem("x_updated")
        hg_con_loaded, pool_steps, sums_ready = sem("hg_con_loaded"), sem("pool_steps"), sem("sums_ready")
        w_pair_made, taps_shared, y_squared, y_sq_used = (sem(n) for n in ("w_pair_made", "taps_shared", "y_squared", "y_sq_used"))
        root_ready, sum_done, second_square, conf_gated = (sem(n) for n in ("root_ready", "sum_done", "second_square", "conf_gated"))
        operand_src, operand_hi, operand_ready = sem("operand_src"), sem("operand_hi"), sem("operand_ready")
        std_ready = sem("std_ready")
        dve_steps, act_steps = sem("dve_steps"), sem("act_steps")
        rel_sum, rel_copied, bias_flipped, bias_made = (sem(n) for n in ("rel_sum", "rel_copied", "bias_flipped", "bias_made"))
        lam_summed, lam_exped, lb_shifted, lb_exped = (sem(n) for n in ("lam_summed", "lam_exped", "lb_shifted", "lb_exped"))
        logits_done, negmax_done, probs_done, attn_done = (sem(n) for n in ("logits_done", "negmax_done", "probs_done", "attn_done"))
        attn_turned, attn_t_done, av_done, da_copied = (sem(n) for n in ("attn_turned", "attn_t_done", "av_done", "da_copied"))
        head_sq, head_mean, head_rstd = sem("head_sq"), sem("head_mean"), sem("head_rstd")
        gate_act, forget_made, log_made, cum_made = (sem(n) for n in ("gate_act", "forget_made", "log_made", "cum_made"))
        cum_exp, kdec_exp, kdec_made = sem("cum_exp"), sem("kdec_exp"), sem("kdec_made")
        kdec_turned, kdec_t_done, diff_made, diff_exp = (sem(n) for n in ("kdec_turned", "kdec_t_done", "diff_made", "diff_exp"))
        level_in, level_mm, level_kept = sem("level_in"), sem("level_mm"), sem("level_kept")
        outer_done, state_made, rec_done, rec_copied = (sem(n) for n in ("outer_done", "state_made", "rec_done", "rec_copied"))
        mlogits_done, mneg_done, mprobs_done, mnormed = (sem(n) for n in ("mlogits_done", "mneg_done", "mprobs_done", "mnormed"))
        mturned, mp_t_done, mpv_done = sem("mturned"), sem("mp_t_done"), sem("mpv_done")
        conv_read, gate_ready, silu_done = sem("conv_read"), sem("gate_ready"), sem("silu_done")
        conf_used, pool_made, pool_mixed = (sem(n) for n in ("conf_used", "pool_made", "pool_mixed"))
        ln_src, ln_mean, ln_centred, ln_sq, ln_var, ln_std, ln_scaled, ln_read = (
            sem(n) for n in ("ln_src", "ln_mean", "ln_centred", "ln_sq", "ln_var", "ln_std", "ln_scaled", "ln_read"))
        shared_ready, stored = sem("shared_ready"), sem("stored")
        shared_added, kk_ready, x_reloaded = sem("shared_added"), sem("kk_ready"), sem("x_reloaded")

        block = ctx.enter_context(nc.Block())

        def attention_steps(slots):
            return {k: t for t, k in enumerate(slots)}

        HOSTS = ("hg_i", 0), ("hg_fm", 0), ("hg_fm", 1), ("hg_fm", 2)
        HOST_PE = [3, 5, 7, 9, 11, 13, 15]
        HOST_EW = [c + 2 for c in HOST_PE]

        def results(parity, i):
            return ps[:, 4 * parity + i].rearrange("p (a t) -> p a t", a=2)

        def run_product(eng, g, split, piece, first=None, extra=None, also=None, slots=None, loops=()):
            base = g.first_chunk // SLOTS
            per = g.chunks // SLOTS

            def one(b, parity):
                static = isinstance(b, int)
                for k in range(SLOTS, g.chunks + SLOTS):
                    if not (g.name == "down_2" and static and b == g.blocks - 1 and k >= g.chunks):
                        split(base + per * b + k // SLOTS, k % SLOTS)
                    if static and b == 0:
                        if first:
                            first(k)
                    else:
                        for i in ([k - SLOTS] if slots is None else slots.get(k, ())):
                            piece(b - 1, i, 1 - parity)
                    if also:
                        also(b, k)
                    if extra and static and b == g.blocks - 1:
                        extra(k)

            one(0, g.first_block % 2)
            last = g.blocks - 1 if extra or also else g.blocks
            pairs = (last - 1) // 2
            if pairs < 2 or also:
                pairs = 0
            if pairs:
                par0 = (g.first_block + 1) % 2
                with eng.Fori(0, pairs) as m:
                    with ExitStack() as inner:
                        for steps, count in loops:
                            inner.enter_context(steps.loop(m, pairs, 2 * count))
                        for d in range(2):
                            one(2 * m + (1 + d), (par0 + d) % 2)
            for b in range(1 + 2 * pairs, g.blocks):
                one(b, (g.first_block + b) % 2)

        def tail(g, piece, at=None):
            last, parity = g.blocks - 1, (g.first_block + g.blocks - 1) % 2

            def go(k):
                for i in ([k - SLOTS] if at is None else at.get(k, ())):
                    piece(last, i, parity)
            return go

        def by_slot(fn, k0, pairs):
            def go(k):
                if 0 <= k - k0 < len(pairs):
                    fn(pairs[k - k0])
            return go

        def both(*fns):
            def go(k):
                for fn in fns:
                    fn(k)
            return go

        def at_slot(slot, fn):
            def go(k):
                if k == slot:
                    fn()
            return go

        def host_banks(host):
            return 4 * ((GM[host[0]].first_block + host[1] + 1) % 2)

        def memory_banks(turn):
            return host_banks(("mem_q", 1)) if turn == 0 else host_banks(("mem_o", 0))

        PAIRS_AT_ONCE = {4: (0, 1), 5: (2, 3)}
        MEM_PE = [2, 3, 4, 6, 7, 8, 10]
        MEM_EW = [4, 5, 6, 8, 9, 10, 12]
        M_SCALE = float(MHT * P) ** -0.5
        CONF_AT = ((1, 8), (2, 4))
        LN_BANKS = (3, 7)

        @block.sync
        def _(sp):
            sp.dma_start(x[:, :, :], A["x"]).then_inc(x_loaded, 16)
            for s in range(SLOTS):
                sp.dma_start(raw[:, s], A["weights"][s]).then_inc(raw_loaded[s], 16)
            with sp.Fori(1, NCHUNK // SLOTS) as i:
                for s in range(SLOTS):
                    sp.wait_ge(chunk_split, SLOTS * i + s - (SLOTS - 1))
                    sp.dma_start(raw[:, s], A["weights"][SLOTS * i + s]).then_inc(raw_loaded[s], 16)

        @block.gpsimd
        def _(pool):
            pool.dma_start(par[:, :], A["params"]).then_inc(params_loaded, 16)
            pool.dma_start(con[:, :], A["consts"]).then_inc(consts_loaded, 16)
            pool.dma_start(lam_in[:, :, :], A["lam"].partition_broadcast(P)).then_inc(consts_loaded, 16)
            pool.dma_start(relb[0:33, :], A["rel_bias"]).then_inc(table_loaded, 16)
            pool.dma_start(onehot[:, :], A["onehot"]).then_inc(table_loaded, 16)
            pool.dma_start(flip[:, :], A["flip"]).then_inc(table_loaded, 16)
            pool.wait_ge(rel_copied, 1)
            pool.dma_start(rel_dram, rel_row[:, :]).then_inc(rel_stored, 16)
            pool.wait_ge(rel_stored, 16)
            shifted = bass.AP(rel_dram.tensor, 0, [[1, P], [NREL, HEADS], [1, TOK]])
            pool.dma_start(rel_rev[:, :, :], shifted).then_inc(rel_loaded, 16)
            steps = Steps(pool, pool_steps)
            TT = nc.gpsimd.tensor_tensor

            def sums(src, ready, pairs=8, weighted=False):
                used = {}
                for j in range(pairs):
                    ready(j)
                    if j >= 2:
                        steps.wait(used[j - 2])
                    t = src[:, 2 * j:2 * j + 2]
                    steps.inc(TT(sqb[:, j % 2] if j else sumsq[:, :, :], t, t, ALU.mult))
                    steps.wait()
                    total = lambda into: TT(into[:, :, :], into[:, :, :], sqb[:, j % 2], ALU.add)
                    if j and not weighted and j == pairs - 1:
                        total(sumsq).then_inc(sums_ready, 1)
                    elif j:
                        steps.inc(total(sumsq))
                    if weighted:
                        for e in range(2):
                            src_, dst_ = (sqb[:, j % 2, e], sqb[:, j % 2, e]) if j else (sumsq[:, e], sumsq_w[:, e])
                            if j and e == 0:
                                steps.wait()
                            steps.inc(nc.gpsimd.tensor_scalar(dst_, src_, w_pair[:, 0, 2 * j + e:2 * j + e + 1], None, ALU.mult))
                        if j:
                            steps.wait()
                            if j == pairs - 1:
                                total(sumsq_w).then_inc(sums_ready, 1)
                            else:
                                steps.inc(total(sumsq_w))
                    used[j] = steps.n

            def of_x(v):
                return lambda j: pool.wait_ge(x_updated, 8 * v + j + 1)

            once = lambda s: (lambda j: pool.wait_ge(s, 16) if j == 0 else None)
            sums(x, once(x_loaded))
            pool.wait_ge(std_ready, STD_END[0])
            pool.dma_start(hg_con[:, :], A["hg_consts"]).then_inc(hg_con_loaded, 16)
            pool.wait_ge(level_in, 6)
            pool.dma_start(x[:, :, :], A["x"]).then_inc(x_reloaded, 16)
            pool.wait_ge(operand_ready, READY["mix_h"] + 4)
            pool.dma_start(mem_x[:, :, :], A["mem"]).then_inc(mem_loaded, 16)
            sums(mem_x, once(mem_loaded))
            pool.wait_ge(std_ready, STD_END[1])
            sums(x, of_x(0))
            pool.wait_ge(std_ready, STD_END[2])
            sums(x, of_x(1))
            pool.wait_ge(operand_ready, READY["down"] + FT)
            sums(x, of_x(2), weighted=True)
            pool.wait_ge(chunk_used, GM["down"].end_chunk)
            pool.dma_start(pw[:, :, :], A["pool_w"]).then_inc(pool_w_loaded, 16)
            pool.wait_ge(taps_shared, 2)
            for tap in range(1, CONF_TAPS):
                pool.wait_ge(shared_ready, tap)
                if tap > 1:
                    pool.wait_ge(shared_added, tap - 1)
                TT(acc[:, 4:6], acc[:, 4:6], hbuf[:, tap % 4], ALU.add).then_inc(shared_added, 1)
            pool.wait_ge(std_ready, STD_END[4])
            half_sums = lambda first: sums(yres, lambda j: pool.wait_ge(act_evac, first + j + 1), 4)
            half_sums(GM["out_2"].first_evac)
            pool.wait_ge(std_ready, STD_END[5])
            sums(x, of_x(4))
            pool.wait_ge(operand_ready, READY["down_2"] + FT)
            half_sums(GM["down_2"].first_evac)
            for j in range(8):
                pool.wait_ge(x_updated, 8 * 5 + j + 1)
                pool.dma_start(A["out"][:, 2 * j:2 * j + 2], x[:, 2 * j:2 * j + 2]).then_inc(stored, 16)
            pool.wait_ge(stored, 8 * 16)

        @block.scalar
        def _(act):
            steps = Steps(act, act_steps)

            def split(u, s):
                act.wait_ge(raw_loaded[s], 16 * u + 16)
                if not isinstance(u, int) or u > 0:
                    act.wait_ge(chunk_used, SLOTS * u + (s - SLOTS + 1))
                nc.scalar.activation(w_hi[:, s], raw[:, s], ACT.Copy).then_inc(hi_rounded, 1)

            def read_out(ins):
                ins.then_inc(act_evac, 1)

            def block_done(g, b):
                act.wait_ge(chunk_used, g.first_chunk + g.chunks * b + g.chunks)

            def nothing(b, i, parity):
                pass

            def take_token_major(g, dst, slot):
                def piece(b, i, parity):
                    if i == 0:
                        block_done(g, b)
                        act.wait_ge(root_ready, STD_END[slot])
                    read_out(nc.scalar.activation(dst(b, i), ps[:, 4 * parity + i], ACT.Copy,
                                                  scale=small[:, 56 + 2 * slot + i // 2:57 + 2 * slot + i // 2]))
                return piece

            def root(n, by_token=False):
                act.wait_ge(sum_done, n + 1)
                slot = STATS[n][1]
                nc.scalar.activation(rstd[:, slot], ps[:, SUM_BANK[n], 0:TOK], ACT.Sqrt, scale=1.0 / DM, bias=cc("eps", 0, 1)).then_inc(std_ready, 1)
                if by_token:
                    nc.scalar.activation(small[:, 56 + 2 * slot:58 + 2 * slot], ps[:, SUM_BANK[n], TOK:TOK + 2], ACT.Sqrt,
                                         scale=1.0 / DM, bias=cc("eps", 0, 1)).then_inc(std_ready, 1)

            def round_pair(j, src, col, ready):
                ready(j)
                for e in range(2):
                    ins = nc.scalar.activation(op_hi[:, 2 * j + e], src[:, 2 * j + e], ACT.Copy, scale=col(2 * j + e))
                ins.then_inc(operand_hi, 1)

            of_weight = lambda name: (lambda t: pc(name, t))
            of_x = lambda v: (lambda j: act.wait_ge(x_updated, 8 * v + j + 1))
            in_pair = lambda j: round_pair(j, x, of_weight("norm_mix_w"), lambda j: act.wait_ge(x_loaded, 16) if j == 0 else None)
            mem_pair = lambda j: round_pair(j, mem_x, of_weight("mem_kv_norm_w"), lambda j: act.wait_ge(mem_loaded, 16) if j == 0 else None)
            mq_pair = lambda j: round_pair(j, x, of_weight("norm_mem_w"), of_x(0))
            up_pair = lambda j: round_pair(j, x, of_weight("norm_ffn_w"), of_x(1))
            in_2_pair = lambda j: round_pair(j, x, lambda t: w_pair[:, 1, t:t + 1], of_x(2))
            up_2_pair = lambda j: round_pair(j, x, of_weight("norm_ffn_pre_2"), of_x(4))

            act.wait_ge(params_loaded, 16)
            split(0, 0)
            split(0, 1)
            in_pair(0)
            split(0, 2)
            in_pair(1)
            split(0, 3)

            def exponents():
                act.wait_ge(lam_summed, 2)
                for i in range(2):
                    nc.scalar.activation(small[:, 2 + i:3 + i], small[:, i:i + 1], ACT.Exp).then_inc(lam_exped, 1)
                act.wait_ge(lb_shifted, 2)
                nc.scalar.activation(small[:, 32:48], small[:, 32:48], ACT.Exp).then_inc(lb_exped, 1)

            def bias_out():
                for j in range(4):
                    act.wait_ge(bias_flipped, j + 1)
                    nc.scalar.activation(bias[:, 2 * j:2 * j + 2], results(1, j), ACT.Copy).then_inc(bias_made, 1)

            def in_root():
                act.wait_ge(consts_loaded, 32)
                root(0, True)

            run_product(act, GM["da_fm"], split, nothing, both(by_slot(in_pair, SLOTS, range(2, 8)), at_slot(11, exponents),
                                                               at_slot(13, bias_out), at_slot(15, in_root)))

            def probs(item):
                qb = item % 2
                act.wait_ge(negmax_done, item + 1)
                nk = P * (qb + 1)
                for m in range(2):
                    nc.scalar.activation(logit[:, item % 2, m, 0:nk], logit[:, item % 2, m, 0:nk], ACT.Exp,
                                         scale=1.0 / BIAS_SCALE, bias=small[:, 8 + 4 * (item % 2) + m:9 + 4 * (item % 2) + m],
                                         accum_out=small[:, 16 + 4 * (item % 2) + m:17 + 4 * (item % 2) + m]).then_inc(probs_done, 1)

            def turn_out(item, bank0):
                qb = item % 2
                act.wait_ge(attn_turned, item + 1)
                if item >= 2:
                    act.wait_ge(av_done, item - 1)
                nk = P * (qb + 1)
                nc.scalar.activation(attn_t[:, item % 2, 0:nk], ps[:, bank0 + 2, 0:nk], ACT.Copy).then_inc(attn_t_done, 1)

            def head_out(h, bank0):
                act.wait_ge(av_done, 2 * h + 2)
                nc.scalar.activation(da_o[:, h], ps[:, bank0 + 3, 0:TOK], ACT.Copy).then_inc(da_copied, 1)

            def attention(host, k):
                if k not in HOST_EW:
                    return
                t, item, bank0 = HOST_EW.index(k), 4 * host, host_banks(HOSTS[host])
                if t < 4:
                    probs(item + t)
                if 2 <= t < 6:
                    turn_out(item + t - 2, bank0)
                if t in (4, 6):
                    head_out((item + t - 4) // 2, bank0)

            run_product(act, GM["da_v"], split, nothing)
            values_out = lambda which: (lambda b, i: tokv[:, which, i // 2, (i % 2) * BANK:(i % 2 + 1) * BANK])
            run_product(act, GM["hg_i"], split, nothing, tail(GM["da_v"], take_token_major(GM["da_v"], values_out(0), 0), PAIRS_AT_ONCE),
                        also=lambda b, k: attention(0, k))
            def beside_hg(b, k):
                attention(1 + b, k)
                if (b, k) == (1, 6):
                    act.wait_ge(dve_evac, GM["hg_fm"].first_evac + 4)
                    nc.scalar.activation(r_kk[:, :, :], proj[:, 8:16], ACT.Sigmoid).then_inc(gate_act, 1)
                if (b, k) == (1, 12):
                    act.wait_ge(forget_made, 1)
                    nc.scalar.activation(r_b[:, :, :], r_a[:, :, :], ACT.Ln).then_inc(log_made, 1)
                if (b, k) == (2, 6):
                    act.wait_ge(cum_made, 1)
                    nc.scalar.activation(r_a[:, :, :], r_c[:, :, :], ACT.Exp).then_inc(cum_exp, 1)
                if (b, k) == (2, 10):
                    act.wait_ge(cum_made, 2)
                    nc.scalar.activation(r_b[:, :, :], r_b[:, :, :], ACT.Exp).then_inc(kdec_exp, 1)

            run_product(act, GM["hg_fm"], split, nothing, tail(GM["hg_i"], take_token_major(GM["hg_i"], values_out(1), 0), PAIRS_AT_ONCE),
                        also=beside_hg)

            def head_square(j, squared, src, ready):
                act.wait_ge(*ready)
                nc.scalar.activation(squared[:, 2 * j:2 * j + 2], src[:, 2 * j:2 * j + 2], ACT.Square).then_inc(head_sq, 1)

            def head_roots(scaled, n, parity):
                for j in range(4):
                    act.wait_ge(head_mean, 4 * n + j + 1)
                    steps.inc(nc.scalar.activation(scaled[:, 2 * j:2 * j + 2], results(parity, j), ACT.Ln, scale=1.0 / P, bias=cc("eps", 0, 1)))
                for j in range(4):
                    steps.wait()
                    nc.scalar.activation(scaled[:, 2 * j:2 * j + 2], scaled[:, 2 * j:2 * j + 2], ACT.Exp, scale=-0.5).then_inc(head_rstd, 1)

            def head_hi(squared, hi_at, stage):
                for j in range(4):
                    act.wait_ge(operand_src, SRC[stage] + j + 1)
                    nc.scalar.activation(op_hi[:, hi_at + 2 * j:hi_at + 2 * j + 2], squared[:, 2 * j:2 * j + 2], ACT.Copy).then_inc(operand_hi, 1)

            for j in range(4):
                head_square(j, da_sq, da_o, (da_copied, 2 * j + 2))
            head_roots(da_rs, 0, 1)

            for j in range(4):
                act.wait_ge(kdec_turned, j + 1)
                nc.scalar.activation(r_f[:, 2 * j:2 * j + 2], ps[:, j].rearrange("p (a t) -> p a t", a=2), ACT.Copy).then_inc(kdec_t_done, 1)
            half = CH // 2
            level = 0
            while half:
                buf = (r_a, r_b)[level % 2]
                act.wait_ge(diff_made, level + 1)
                v = buf[:, :, :].rearrange("p h t -> p (h t)").rearrange("p (n s k) -> p n s k", s=2, k=half)
                nc.scalar.activation(v[:, :, 0], v[:, :, 0], ACT.Exp, scale=-1.0).then_inc(diff_exp, 1)
                nc.scalar.activation(v[:, :, 1], v[:, :, 1], ACT.Exp).then_inc(diff_exp, 1)
                half //= 2
                level += 1
                if level == 2:
                    head_hi(da_sq[:, :, :], 0, "mix_a")
                if level == 3:
                    act.wait_ge(dve_evac, GM["hg_fm"].end_evac)
                    nc.scalar.activation(proj[:, 16:24], proj[:, 16:24], ACT.Silu).then_inc(gate_act, 1)
            def rec_out(j):
                act.wait_ge(rec_done, j + 1)
                if j == 0:
                    act.wait_ge(level_mm, 7)
                nc.scalar.activation(r_e[:, 2 * j:2 * j + 2], results(0, j), ACT.Copy).then_inc(rec_copied, 1)
                head_square(j, r_j, r_e, (rec_copied, j + 1))

            def beside_out(k):
                if k in (5, 6):
                    rec_out(2 * k - 10)
                    rec_out(2 * k - 9)
                if k == 6:
                    head_roots(r_f, 1, 0)
                if k == 7:
                    head_hi(r_j[:, :, :], 8, "mix_h")

            run_product(act, GM["out"], split, nothing, beside_out, extra=by_slot(mem_pair, 12, range(4)))
            run_product(act, GM["mem_k"], split, nothing, both(by_slot(mem_pair, SLOTS, range(4, 8)), at_slot(14, lambda: root(1, True))))
            mv_out = take_token_major(GM["mem_v"], lambda b, i: mv[:, i // 2, CW * b + (i % 2) * BANK:CW * b + (i % 2 + 1) * BANK], 1)
            run_product(act, GM["mem_v"], split, mv_out, slots=PAIRS_AT_ONCE, extra=by_slot(mq_pair, 12, range(4)))

            def memory_attention(turn, t):
                bank0 = memory_banks(turn)
                if t < 4:
                    item = 4 * turn + t
                    act.wait_ge(mneg_done, item + 1)
                    nc.scalar.activation(mp[:, item % 2], ps[:, bank0, 0:TOK], ACT.Exp, scale=M_SCALE,
                                         bias=small[:, 8 + item % 2:9 + item % 2],
                                         accum_out=small[:, 16 + item % 2:17 + item % 2]).then_inc(mprobs_done, 1)
                if 2 <= t < 6:
                    it = 4 * turn + t - 2
                    h, qb = divmod(it, 2)
                    act.wait_ge(mturned, it + 1)
                    if h >= 2:
                        act.wait_ge(mpv_done, 2 * (h - 1))
                    nc.scalar.activation(mp_t[:, h % 2, :, qb * P:(qb + 1) * P],
                                         ps[:, bank0 + 1, 0:TOK].rearrange("p (k t) -> p k t", k=2), ACT.Copy).then_inc(mp_t_done, 1)
                if t in (4, 6):
                    for j in range(2):
                        q = 2 * (2 * turn + (t - 4) // 2) + j
                        act.wait_ge(mpv_done, q + 1)
                        nc.scalar.activation(op_hi[:, 2 * q:2 * q + 2], ps[:, bank0 + 2 + j].rearrange("p (a t) -> p a t", a=2), ACT.Copy).then_inc(operand_hi, 1)

            run_product(act, GM["mem_q"], split, nothing,
                        both(tail(GM["mem_v"], mv_out, PAIRS_AT_ONCE), by_slot(mq_pair, SLOTS, range(4, 8)), at_slot(14, lambda: root(2))),
                        extra=lambda k: memory_attention(0, HOST_EW.index(k)) if k in HOST_EW else None)
            run_product(act, GM["mem_o"], split, nothing, lambda k: memory_attention(1, MEM_EW.index(k)) if k in MEM_EW else None,
                        extra=by_slot(up_pair, 12, range(4)))

            def feed_forward(g, gd, turn):
                q0, s0 = READY[gd.name], SRC[gd.name]

                def piece(b, i, parity):
                    if 1 <= i < 5:
                        p = i - 1
                        act.wait_ge(gate_ready, turn * 4 * g.blocks + 4 * b + p + 1)
                        nc.scalar.activation(cg[:, p % 2], cg[:, p % 2], ACT.Silu).then_inc(silu_done, 1)
                    if 2 <= i < 6:
                        p = i - 2
                        act.wait_ge(operand_src, s0 + 4 * b + p + 1)
                        nc.scalar.activation(g_hi[:, bass.ds(4 * b + p, 1)], cv[:, bass.ds(p % 2, 1)], ACT.Copy).then_inc(operand_hi, 1)
                return piece

            gate = feed_forward(GM["up"], GM["down"], 0)
            ffn_slots = {SLOTS + 2 * i: (i,) for i in range(6)}
            run_product(act, GM["up"], split, gate, both(by_slot(up_pair, SLOTS, range(4, 8)), at_slot(14, lambda: root(3))), slots=ffn_slots)
            run_product(act, GM["down"], split, nothing, tail(GM["up"], gate, ffn_slots), extra=by_slot(in_2_pair, 12, range(4)))

            def two_roots():
                root(4)
                act.wait_ge(second_square, 1)
                nc.scalar.activation(rstd[:, 1], rstd[:, 1], ACT.Sqrt, scale=1.0 / DM, bias=cc("eps", 0, 1)).then_inc(std_ready, 1)

            def conf_gate(b):
                act.wait_ge(dve_evac, GM["conf"].first_evac + 2 * b + 2)
                nc.scalar.activation(ub[:, 1], ub[:, 1], ACT.Sigmoid).then_inc(conf_gated, 1)

            def beside_conf(b, k):
                if (b, k) == (1, 6):
                    two_roots()
                if (b, k) in CONF_AT:
                    conf_gate(b - 1)

            run_product(act, GM["conf"], split, nothing, by_slot(in_2_pair, SLOTS + 1, range(4, 8)), also=beside_conf)
            shared = list(range(1, CONF_TAPS))

            def shared_taps(n):
                for tap in shared[:n]:
                    if tap == 1:
                        act.wait_ge(conf_used, 3)
                    if tap > 4:
                        act.wait_ge(shared_added, tap - 4)
                    for e in range(2):
                        ins = nc.scalar.activation(hbuf[:, tap % 4, e], glu[:, 4 + e, tap:tap + TOK], ACT.Copy, scale=pc("conv_b_w_2", 6 * tap + 4 + e))
                    ins.then_inc(shared_ready, 1)
                del shared[:n]

            run_product(act, GM["pool"], split, nothing, both(at_slot(SLOTS, lambda: conf_gate(2)), lambda k: shared_taps(2) if k > 6 else None))

            def gated_hi(b):
                act.wait_ge(operand_src, SRC["gated"] + b + 1)
                nc.scalar.activation(y_hi[:, 10 + 2 * b:12 + 2 * b], ya[:, :, :], ACT.Copy).then_inc(operand_hi, 1)

            def pool_out():
                act.wait_ge(pool_mixed, 1)
                for i in range(4):
                    steps.inc(nc.scalar.activation(pa[:, i, PPAD:PPAD + TOK], ps[:, 3 + 4 * (i // 2), (i % 2) * TOK:(i % 2 + 1) * TOK], ACT.Copy,
                                                   scale=pc("pool_scale_2", i)))
                for j in range(2):
                    steps.wait(steps.n - 2 + 2 * j)
                    nc.scalar.activation(y_hi[:, 2 * j:2 * j + 2], pa[:, 2 * j:2 * j + 2, PPAD:PPAD + TOK], ACT.Copy).then_inc(operand_hi, 1)

            def beside_gated(b, k):
                shared_taps(2)
                if (b, k) == (1, 5):
                    pool_out()
                if (b, k) == (1, 8):
                    gated_hi(0)
                if (b, k) == (2, 9):
                    act.wait_ge(ln_centred, 1)
                    nc.scalar.activation(lnz[:, :, :], acc[:, :, :], ACT.Square).then_inc(ln_sq, 1)
                if (b, k) == (2, 11):
                    act.wait_ge(ln_var, 1)
                    nc.scalar.activation(hbuf[:, 0, 1], ps[:, LN_BANKS[1], 0:TOK], ACT.Sqrt, scale=1.0 / WB, bias=cc("eps", 1, 1)).then_inc(ln_std, 1)
                if (b, k) == (2, 13):
                    act.wait_ge(ln_scaled, 1)
                    for i in range(6):
                        steps.inc(nc.scalar.activation(lnz[:, i], acc[:, i], ACT.Silu, scale=pc("ln_b_gain_2", i), bias=pc("ln_b_bias_2", i)))
                if (b, k) == (2, 14):
                    for j in range(3):
                        steps.wait(steps.n - 4 + 2 * j)
                        nc.scalar.activation(y_hi[:, 4 + 2 * j:6 + 2 * j], lnz[:, 2 * j:2 * j + 2], ACT.Copy).then_inc(operand_hi, 1)
                if (b, k) == (2, 15):
                    gated_hi(1)

            run_product(act, GM["gated"], split, nothing, also=beside_gated)

            def take_y(g):
                def piece(b, i, parity):
                    if i == 0:
                        block_done(g, b)
                    read_out(nc.scalar.activation(yres[:, 8 * b + 2 * i:8 * b + 2 * i + 2], results(parity, i), ACT.Copy))
                return piece

            def last_y(g, turn):
                piece, parity = take_y(g), (g.first_block + 1) % 2
                block_done(g, 1)
                for i in range(4):
                    nc.scalar.activation(hbuf[:, i], results(parity, i), ACT.Square).then_inc(y_squared, 1)
                for i in range(4):
                    piece(1, i, parity)
                root(5 + 2 * turn)

            y_slots = {SLOTS + i: (i,) for i in range(4)}
            run_product(act, GM["out_2"], split, take_y(GM["out_2"]), at_slot(6, lambda: gated_hi(2)), slots=y_slots)
            last_y(GM["out_2"], 0)
            for j in range(4):
                up_2_pair(j)
            gate = feed_forward(GM["up_2"], GM["down_2"], 1)
            run_product(act, GM["up_2"], split, gate, both(by_slot(up_2_pair, SLOTS, range(4, 8)), at_slot(14, lambda: root(6))), slots=ffn_slots)
            run_product(act, GM["down_2"], split, take_y(GM["down_2"]), tail(GM["up_2"], gate, ffn_slots), slots=y_slots)
            last_y(GM["down_2"], 1)

        @block.vector
        def _(dve):
            steps = Steps(dve, dve_steps)
            upd = Steps(dve, x_updated)
            STT = nc.vector.scalar_tensor_tensor
            TT = nc.vector.tensor_tensor
            TS = nc.vector.tensor_scalar

            def split(u, s):
                dve.wait_ge(hi_rounded, SLOTS * u + (s + 1))
                TT(w_lo[:, s], raw[:, s], w_hi[:, s].bitcast(F32), ALU.subtract).then_inc(chunk_split, 1)

            def nothing(b, i, parity):
                pass

            def block_done(g, b):
                dve.wait_ge(chunk_used, g.first_chunk + g.chunks * b + g.chunks)

            def add_to_x(g):
                def piece(b, i, parity):
                    if i == 0:
                        block_done(g, b)
                    t = x[:, 8 * b + 2 * i:8 * b + 2 * i + 2]
                    upd.inc(TT(t, results(parity, i), t, ALU.add))
                return piece

            def scale_out(dst, parity, i, slot):
                TT(dst, results(parity, i), spread(rstd[:, slot], 2), ALU.mult).then_inc(dve_evac, 1)

            def take(g, dst, slot):
                def piece(b, i, parity):
                    if i == 0:
                        block_done(g, b)
                    scale_out(dst(b, i), parity, i, slot)
                return piece

            def inverse_root(n, by_token=False):
                slot = STATS[n][1]
                dve.wait_ge(std_ready, STD_END[n] - (1 if n == 4 else 0))
                nc.vector.reciprocal(rstd[:, slot], rstd[:, slot]).then_inc(root_ready, 1)
                if by_token:
                    nc.vector.reciprocal(small[:, 56 + 2 * slot:58 + 2 * slot], small[:, 56 + 2 * slot:58 + 2 * slot]).then_inc(root_ready, 1)
                dve.wait_ge(root_ready, STD_END[n] - (1 if n == 4 else 0))

            def rest_of(hi, lo, src, q):
                dve.wait_ge(operand_hi, q + 1)
                TT(lo, src, hi.bitcast(F32), ALU.subtract).then_inc(operand_ready, 1)

            def low_pair(stage, src, col):
                def go(j):
                    dve.wait_ge(operand_hi, READY[stage] + j + 1)
                    for e in range(2):
                        t = 2 * j + e
                        ins = STT(op_lo[:, t], src[:, t], col(t), op_hi[:, t].bitcast(F32), ALU.mult, ALU.subtract)
                    ins.then_inc(operand_ready, 1)
                return go

            of_weight = lambda name: (lambda t: pc(name, t))
            in_pair = low_pair("in", x, of_weight("norm_mix_w"))
            mem_pair = low_pair("mem", mem_x, of_weight("mem_kv_norm_w"))
            mq_pair = low_pair("mem_q", x, of_weight("norm_mem_w"))
            up_pair = low_pair("up", x, of_weight("norm_ffn_w"))
            in_2_pair = low_pair("in_2", x, lambda t: w_pair[:, 1, t:t + 1])
            up_2_pair = low_pair("up_2", x, of_weight("norm_ffn_pre_2"))

            dve.wait_ge(params_loaded, 16)
            split(0, 0)
            split(0, 1)
            in_pair(0)
            split(0, 2)
            in_pair(1)
            split(0, 3)

            def table_out():
                dve.wait_ge(rel_sum, 1)
                nc.vector.tensor_copy(rel_row[:, :], ps[0:HEADS, 4, 0:NREL]).then_inc(rel_copied, 1)

            raw0, raw1 = pc("hg_lb_raw", 0, 8), pc("hg_lb_raw", 8, 8)

            def scalars():
                dve.wait_ge(consts_loaded, 32)
                for i in range(2):
                    nc.vector.tensor_tensor_reduce(out=hbuf[:, i, 0, 0:64], in0=lam_in[:, 2 * i], in1=lam_in[:, 2 * i + 1], scale=1.0, scalar=0.0,
                                                   op0=ALU.mult, op1=ALU.add, accum_out=small[:, i:i + 1]).then_inc(lam_summed, 1)
                steps.inc(TT(small[:, 48:56], raw0, raw1, ALU.max))
                steps.wait()
                TT(small[:, 32:40], raw0, small[:, 48:56], ALU.subtract).then_inc(lb_shifted, 1)
                TT(small[:, 40:48], raw1, small[:, 48:56], ALU.subtract).then_inc(lb_shifted, 1)
                w1, w2 = pc("final_norm_w", 0, KT), pc("norm_mix_pre_2", 0, KT)
                TT(w_pair[:, 0], w1, w1, ALU.mult).then_inc(w_pair_made, 1)
                TT(w_pair[:, 1], w1, w2, ALU.mult).then_inc(w_pair_made, 1)

            def scalars_on():
                dve.wait_ge(lam_exped, 2)
                steps.inc(TT(small[:, 4:5], small[:, 3:4], small[:, 2:3], ALU.subtract))
                steps.wait()
                steps.inc(nc.vector.memset(small[:, 5:6], 1.0))
                steps.inc(TS(small[:, 6:7], small[:, 4:5], -LAM_INIT, None, ALU.add))
                steps.inc(TS(small[:, 7:8], pc("da_subln_w"), 1.0 - LAM_INIT, None, ALU.mult))
                dve.wait_ge(lb_exped, 1)
                steps.inc(TT(small[:, 48:56], small[:, 32:40], small[:, 40:48], ALU.add))
                steps.wait()
                steps.inc(nc.vector.reciprocal(small[:, 48:56], small[:, 48:56]))
                steps.wait()
                steps.inc(TT(small[:, 32:40], small[:, 32:40], small[:, 48:56], ALU.mult))
                steps.wait()
                steps.inc(TS(small[:, 40:48], small[:, 32:40], -1.0, 1.0, ALU.mult, ALU.add))
                steps.wait()

            run_product(dve, GM["da_fm"], split, take(GM["da_fm"], lambda b, i: proj[:, 24 + 8 * b + 2 * i:26 + 8 * b + 2 * i], 0),
                        both(by_slot(in_pair, SLOTS, range(2, 8)), at_slot(5, table_out), at_slot(10, scalars), at_slot(12, scalars_on),
                             at_slot(16, lambda: inverse_root(0, True))), slots={SLOTS + i: (i,) for i in range(4)})

            def softmax_top(item, bank0):
                qb = item % 2
                nk = P * (qb + 1)
                dve.wait_ge(logits_done, item + 1)
                if item == 0:
                    dve.wait_ge(bias_made, 4)
                if item >= 2:
                    dve.wait_ge(attn_done, item - 1)
                h = item // 2
                lg = logit[:, item % 2, :, 0:nk]
                t = steps.inc(TT(lg, ps[:, bank0:bank0 + 2, 0:nk],
                                 spread(bias[:, h, TOK - nk:TOK], 2), ALU.add))
                steps.wait(t)
                c = 8 + 4 * (item % 2)
                t = steps.inc(nc.vector.reduce_max(small[:, c + 2:c + 4], lg, AX))
                steps.wait(t)
                TS(small[:, c:c + 2], small[:, c + 2:c + 4], -1.0 / BIAS_SCALE, None, ALU.mult).then_inc(negmax_done, 1)

            def softmax_mix(item):
                qb = item % 2
                nk = P * (qb + 1)
                dve.wait_ge(probs_done, 2 * item + 2)
                c = 16 + 4 * (item % 2)
                t = steps.inc(nc.vector.reciprocal(small[:, c + 2:c + 4], small[:, c:c + 2]))
                steps.wait(t)
                t = steps.inc(TT(small[:, c + 2:c + 4], small[:, c + 2:c + 4], small[:, 5:7], ALU.mult))
                steps.wait(t)
                if item >= 2:
                    dve.wait_ge(attn_turned, item - 1)
                a = attn[:, item % 2, 0:nk]
                t = steps.inc(TS(a, logit[:, item % 2, 0, 0:nk], small[:, c + 2:c + 3], None, ALU.mult))
                steps.wait(t)
                STT(a, logit[:, item % 2, 1, 0:nk], small[:, c + 3:c + 4], a, ALU.mult, ALU.add).then_inc(attn_done, 1)

            def attention(host, k):
                if k not in HOST_EW:
                    return
                t, item = HOST_EW.index(k), 4 * host
                if t < 4:
                    softmax_top(item + t, host_banks(HOSTS[host]))
                if 1 <= t < 5:
                    softmax_mix(item + t - 1)

            four = {SLOTS + i: (i,) for i in range(4)}
            da_out = take(GM["da_fm"], lambda b, i: proj[:, 24 + 8 * b + 2 * i:26 + 8 * b + 2 * i], 0)
            run_product(dve, GM["da_v"], split, nothing, tail(GM["da_fm"], da_out, four))
            run_product(dve, GM["hg_i"], split, nothing, also=lambda b, k: attention(0, k))
            hg_at = (8, 0, 16)
            hg_out = take(GM["hg_fm"], lambda b, i: proj[:, hg_at[b] + 2 * i:hg_at[b] + 2 * i + 2], 0)
            def beside_hg(b, k):
                attention(1 + b, k)
                if (b, k) in ((1, 8), (1, 10)):
                    if k == 8:
                        dve.wait_ge(gate_act, 1)
                        dve.wait_ge(operand_ready, READY["in"] + 8)
                    for h in range(4) if k == 8 else range(4, HEADS):
                        ins = TS(r_a[:, h], r_kk[:, h], small[:, 40 + h:41 + h], small[:, 32 + h:33 + h], ALU.mult, ALU.add)
                    if k == 10:
                        ins.then_inc(forget_made, 1)
                if (b, k) == (1, 14):
                    dve.wait_ge(forget_made, 1)
                    TS(r_kk[:, :, :], r_a[:, :, :], -1.0, 1.0, ALU.mult, ALU.add).then_inc(kk_ready, 1)
                if (b, k) == (1, 18):
                    dve.wait_ge(log_made, 1)
                    dve.wait_ge(hg_con_loaded, 16)
                    for h in range(HEADS):
                        ins = nc.vector.tensor_tensor_scan(r_c[:, h], hg_con[:, CARRY:CARRY + TOK], r_b[:, h], 0.0, ALU.mult, ALU.add)
                    ins.then_inc(cum_made, 1)
                if (b, k) == (2, 8):
                    dve.wait_ge(cum_made, 1)
                    cum = r_c[:, :, :].rearrange("p h t -> p (h t)").rearrange("p (n c) -> p n c", c=CH)
                    TT(r_b[:, :, :].rearrange("p h t -> p (h t)").rearrange("p (n c) -> p n c", c=CH),
                       stretch(cum[:, :, CH - 1], CH), cum, ALU.subtract).then_inc(cum_made, 1)

            run_product(dve, GM["hg_fm"], split, hg_out, slots=PAIRS_AT_ONCE, also=beside_hg)
            for i in range(4):
                hg_out(2, i, (GM["hg_fm"].first_block + 2) % 2)

            dve.wait_ge(cum_exp, 1)
            dve.wait_ge(av_done, 2 * HEADS)
            steps.inc(nc.vector.tensor_copy(decay[:, :, :], r_a[:, :, :].rearrange("p h (c k) -> p h c k", k=CH)[:, :, :, CH - 1]))
            dve.wait_ge(kdec_exp, 1)
            dve.wait_ge(kk_ready, 1)
            TT(r_e[:, :, :], r_kk[:, :, :], r_b[:, :, :], ALU.mult).then_inc(kdec_made, 1)
            dve.wait_ge(dve_evac, GM["hg_fm"].end_evac)
            qe_made = steps.inc(TT(r_d[:, :, :], proj[:, 0:8], r_a[:, :, :], ALU.mult))

            def head_norm(src, out, weight, scaled, n, gate=None):
                for j in range(4):
                    dve.wait_ge(head_rstd, 4 * n + j + 1)
                    sl = slice(2 * j, 2 * j + 2)
                    if gate is None:
                        STT(out[:, sl], src[:, sl], weight, scaled[:, sl], ALU.mult, ALU.mult).then_inc(operand_src, 1)
                    else:
                        steps.inc(STT(out[:, sl], src[:, sl], weight, scaled[:, sl], ALU.mult, ALU.mult))
                        steps.wait()
                        TT(out[:, sl], out[:, sl], gate[:, sl], ALU.mult).then_inc(operand_src, 1)

            def head_low(out, at0, stage):
                for j in range(4):
                    rest_of(op_hi[:, at0 + 2 * j:at0 + 2 * j + 2], op_lo[:, at0 + 2 * j:at0 + 2 * j + 2], out[:, 2 * j:2 * j + 2], READY[stage] + j)

            cleared = steps.inc(nc.vector.memset(r_h[:, :, :], 0.0))

            def keep(level):
                dve.wait_ge(level_mm, level + 1)
                if level:
                    dve.wait_ge(level_kept, level)
                else:
                    steps.wait(cleared)
                mask = hg_con[:, LEVELS + level * P:LEVELS + (level + 1) * P].bitcast(U32)
                (nc.vector.copy_predicated(r_h[:, :, :].rearrange("p h t -> p (h t)").rearrange("p (n t) -> p n t", t=P), spread(mask, 2 * HEADS),
                                                    ps[:, 4 * (level % 2):4 * (level % 2) + 4].rearrange("p b t -> p (b t)").rearrange("p (n t) -> p n t", t=P))).then_inc(level_kept, 1)
            halves = [CH >> (level + 1) for level in range(6)]

            def flat(buf, half):
                return buf.rearrange("p h t -> p (h t)").rearrange("p (n s k) -> p n s k", s=2, k=half)

            def difference(level):
                half, buf = halves[level], (r_a, r_b)[level % 2]
                whole = lambda ap: ap.rearrange("p h t -> p (h t)").rearrange("p (n k) -> p n k", k=2 * half)
                if level == 0:
                    steps.wait(qe_made)
                if level == 1:
                    dve.wait_ge(kdec_made, 1)
                if level >= 2:
                    dve.wait_ge(level_in, level - 1)
                TT(whole(buf[:, :, :]), whole(r_c[:, :, :]), stretch(flat(r_c[:, :, :], half)[:, :, 0, half - 1], 2 * half), ALU.subtract).then_inc(diff_made, 1)

            def level_operand(level):
                half, buf, dst = halves[level], (r_a, r_b)[level % 2], (r_j, r_e)[level % 2]
                if level == 1:
                    dve.wait_ge(kdec_turned, 4)
                if level >= 2:
                    dve.wait_ge(level_mm, level - 1)
                dve.wait_ge(diff_exp, 2 * level + 2)
                TT(flat(dst[:, :, :], half)[:, :, 0], flat(r_kk[:, :, :], half)[:, :, 0], flat(buf[:, :, :], half)[:, :, 0], ALU.mult)
                TT(flat(dst[:, :, :], half)[:, :, 1], flat(proj[:, 0:8], half)[:, :, 1], flat(buf[:, :, :], half)[:, :, 1], ALU.mult).then_inc(level_in, 1)

            difference(0)
            difference(1)
            head_norm(da_o, da_sq, small[:, 7:8], da_rs, 0)
            dve.wait_ge(operand_src, SRC["mix_a"] + 4)
            for level in range(6):
                level_operand(level)
                if level == 1:
                    head_low(da_sq, 0, "mix_a")
                if level >= 1:
                    keep(level - 1)
                if level < 4:
                    difference(level + 2)
            keep(5)
            keep(6)
            dve.wait_ge(operand_ready, READY["mix_a"] + 4)
            for c in range(NCHK - 1):
                dve.wait_ge(outer_done, c + 1)
                if c:
                    dve.wait_ge(state_made, c)
                for h in range(HEADS):
                    u = ps[:, 2 * (c % 2) + h // 4, (h % 4) * P:(h % 4 + 1) * P]
                    if c == 0:
                        ins = nc.vector.tensor_copy(state[:, 0, h], u)
                    else:
                        ins = STT(state[:, c, h], state[:, c - 1, h], decay[:, h, c:c + 1], u, ALU.mult, ALU.add)
                ins.then_inc(state_made, 1)

            def beside_out(k):
                if k == 7:
                    head_norm(r_e, r_j, pc("hg_norm_w"), r_f, 1, proj[:, 16:24])
                if k == 8:
                    head_low(r_j, 8, "mix_h")
                    dve.wait_ge(x_reloaded, 16)

            run_product(dve, GM["out"], split, add_to_x(GM["out"]), beside_out, slots=four, extra=by_slot(mem_pair, 12, range(4)))
            mk_out = take(GM["mem_k"], lambda b, i: mk[:, 8 * b + 2 * i:8 * b + 2 * i + 2], 1)
            run_product(dve, GM["mem_k"], split, mk_out, slots=four,
                        first=both(tail(GM["out"], add_to_x(GM["out"]), four), by_slot(mem_pair, SLOTS, range(4, 8)),
                                   at_slot(15, lambda: inverse_root(1, True))))
            run_product(dve, GM["mem_v"], split, nothing, tail(GM["mem_k"], mk_out, four), extra=by_slot(mq_pair, 12, range(4)))

            def memory_attention(turn, t):
                bank0 = memory_banks(turn)
                if t < 4:
                    item = 4 * turn + t
                    dve.wait_ge(mlogits_done, item + 1)
                    if item >= 2:
                        dve.wait_ge(mnormed, item - 1)
                    n = steps.inc(nc.vector.reduce_max(small[:, 12 + item % 2:13 + item % 2], ps[:, bank0, 0:TOK], AX))
                    steps.wait(n)
                    TS(small[:, 8 + item % 2:9 + item % 2], small[:, 12 + item % 2:13 + item % 2], -M_SCALE, None, ALU.mult).then_inc(mneg_done, 1)
                if 1 <= t < 5:
                    it = 4 * turn + t - 1
                    dve.wait_ge(mprobs_done, it + 1)
                    n = steps.inc(nc.vector.reciprocal(small[:, 20 + it % 2:21 + it % 2], small[:, 16 + it % 2:17 + it % 2]))
                    steps.wait(n)
                    TS(mp[:, it % 2], mp[:, it % 2], small[:, 20 + it % 2:21 + it % 2], None, ALU.mult).then_inc(mnormed, 1)
                if t in (4, 6):
                    for j in range(2):
                        q = 2 * (2 * turn + (t - 4) // 2) + j
                        rest_of(op_hi[:, 2 * q:2 * q + 2], op_lo[:, 2 * q:2 * q + 2], ps[:, bank0 + 2 + j].rearrange("p (a t) -> p a t", a=2), READY["mem_o"] + q)

            mq_out = take(GM["mem_q"], lambda b, i: mq[:, 8 * b + 2 * i:8 * b + 2 * i + 2], 0)
            run_product(dve, GM["mem_q"], split, mq_out, slots=PAIRS_AT_ONCE,
                        first=both(by_slot(mq_pair, SLOTS, range(4, 8)), at_slot(15, lambda: inverse_root(2))),
                        extra=lambda k: memory_attention(0, HOST_EW.index(k)) if k in HOST_EW else None)
            run_product(dve, GM["mem_o"], split, add_to_x(GM["mem_o"]), slots=four,
                        first=both(tail(GM["mem_q"], mq_out, {4: (0, 1, 2, 3)}), lambda k: memory_attention(1, MEM_EW.index(k)) if k in MEM_EW else None),
                        extra=by_slot(up_pair, 12, range(4)))

            def feed_forward(g, gd, turn, w, bname):
                q0 = READY[gd.name]

                def col(name, tap, t, b):
                    return par[:, bass.ds(PCOL[name] + tap * 2 * FT + t + 4 * b, 1)]

                def piece(b, i, parity):
                    if 2 <= i < 6:
                        p = i - 2
                        dve.wait_ge(operand_hi, q0 + 4 * b + p + 1)
                        TT(g_lo[:, bass.ds(4 * b + p, 1)], cv[:, bass.ds(p % 2, 1)], g_hi[:, bass.ds(4 * b + p, 1)].bitcast(F32), ALU.subtract).then_inc(operand_ready, 1)
                    if 1 <= i < 5:
                        p = i - 1
                        dve.wait_ge(silu_done, turn * 4 * g.blocks + 4 * b + p + 1)
                        dve.wait_ge(conv_read, turn * (4 * g.blocks + 4) + 4 * b + p + 5)
                        TT(cv[:, p % 2], cg[:, p % 2], cv[:, p % 2], ALU.mult).then_inc(operand_src, 1)
                    if i < 2:
                        if i == 0:
                            block_done(g, b)
                        dve.wait_ge(conv_read, turn * (4 * g.blocks + 4) + 4 * b + 2 * i + 2)
                        for bank in (i, 2 + i):
                            scale_out(up[:, 2 * bank:2 * bank + 2, UPAD:UPAD + TOK], parity, bank, 1)
                    if i < 4:
                        p = i
                        dve.wait_ge(dve_evac, g.first_evac + 4 * b + 2 * (p // 2) + 2)
                        tiles = ((cg, p, p), (cv, 4 + p, FT + p))
                        dve.wait_ge(operand_ready, q0 + 4 * b + p - 1)
                        ts = []
                        for buf, s, c in tiles:
                            ts.append(steps.inc(TS(buf[:, p % 2], up[:, s, 2:2 + TOK], col(w, 2, c, b), par[:, bass.ds(PCOL[bname] + c + 4 * b, 1)],
                                                   ALU.mult, ALU.add)))
                        for tap in (1, 0):
                            for n, (buf, s, c) in enumerate(tiles):
                                steps.wait(ts[n])
                                ins = STT(buf[:, p % 2], up[:, s, tap:tap + TOK], col(w, tap, c, b), buf[:, p % 2], ALU.mult, ALU.add)
                                if tap:
                                    ts[n] = steps.inc(ins)
                                elif n == 0:
                                    ins.then_inc(gate_ready, 1)
                                else:
                                    ins.then_inc(conv_read, 1)
                def zeros():
                    dve.wait_ge(operand_ready, q0)
                    upd.wait()
                    nc.vector.memset(up[:, :, 0:UPAD], 0.0).then_inc(conv_read, 4)
                return piece, zeros

            ffn_slots = {SLOTS + 2 * i: (i,) for i in range(6)}
            conv, zeros = feed_forward(GM["up"], GM["down"], 0, "conv_w", "conv_b")
            run_product(dve, GM["up"], split, conv, slots=ffn_slots, loops=((steps, 16),),
                        first=both(tail(GM["mem_o"], add_to_x(GM["mem_o"]), four), by_slot(up_pair, SLOTS, range(4, 8)),
                                   at_slot(9, zeros), at_slot(15, lambda: inverse_root(3))))
            run_product(dve, GM["down"], split, add_to_x(GM["down"]), tail(GM["up"], conv, ffn_slots), slots=four,
                        extra=by_slot(in_2_pair, 12, range(4)))

            def two_roots():
                inverse_root(4)
                steps.inc(TT(rstd[:, 1], rstd[:, 0], rstd[:, 0], ALU.mult))
                steps.wait()
                TT(rstd[:, 1], rstd[:, 1], ps[:, SUM_BANK[4], TOK:2 * TOK], ALU.mult).then_inc(second_square, 1)
                dve.wait_ge(std_ready, STD_END[4])
                nc.vector.reciprocal(rstd[:, 1], rstd[:, 1]).then_inc(root_ready, 1)
                dve.wait_ge(root_ready, STD_END[4])
                steps.inc(TT(rstd[:, 1], rstd[:, 1], rstd[:, 0], ALU.mult))
                steps.wait()

            def margins():
                steps.inc(nc.vector.memset(glu[:, :, 0:GPAD], 0.0))
                steps.inc(nc.vector.memset(cvp[:, :, 0:UPAD], 0.0))
                for buf in (px, pa, pb):
                    steps.inc(nc.vector.memset(buf[:, :, 0:PPAD], 0.0))
                steps.wait()

            def conf_out(b):
                g = GM["conf"]
                block_done(g, b)
                if b:
                    dve.wait_ge(conf_used, b)
                for i in range(2):
                    scale_out(ub[:, i], (g.first_block + b) % 2, i, 1)

            def conf_glu(b):
                dve.wait_ge(conf_gated, b + 1)
                TT(glu[:, 2 * b:2 * b + 2, GPAD:GPAD + TOK], ub[:, 0], ub[:, 1], ALU.mult).then_inc(conf_used, 1)

            def tap_of(tap, i):
                w = pc("conv_b_w_2", 6 * tap + i)
                if tap == 0:
                    return TS(acc[:, i], glu[:, i, 0:TOK], w, pc("conv_b_bias_2", i), ALU.mult, ALU.add)
                return STT(acc[:, i], glu[:, i, tap:tap + TOK], w, acc[:, i], ALU.mult, ALU.add)

            todo = [(pair, tap, 2 * pair + e) for pair in range(2) for tap in range(CONF_TAPS) for e in range(2)]
            tap_done = {}

            def some_taps(n):
                for pair, tap, i in todo[:n]:
                    if tap == 0:
                        dve.wait_ge(conf_used, pair + 1)
                    else:
                        steps.wait(tap_done[i])
                    ins = tap_of(tap, i)
                    if tap < CONF_TAPS - 1:
                        tap_done[i] = steps.inc(ins)
                    else:
                        ins.then_inc(ln_src, 1)
                del todo[:n]

            def share_taps():
                dve.wait_ge(conf_used, 3)
                for i in (4, 5):
                    tap_of(0, i).then_inc(taps_shared, 1)

            def beside_conf(b, k):
                if (b, k) == (1, 6):
                    two_roots()
                if (b, k) in CONF_AT:
                    conf_out(b - 1)
                if (b, k - 1) in CONF_AT:
                    conf_glu(b - 1)
                if (b == 1 and k > 9) or (b == 2 and k > 5):
                    some_taps(4)

            run_product(dve, GM["conf"], split, nothing, also=beside_conf,
                        first=both(tail(GM["down"], add_to_x(GM["down"]), four), by_slot(in_2_pair, SLOTS + 1, range(4, 8)),
                                   at_slot(10, margins)))
            run_product(dve, GM["pool"], split, nothing,
                        both(at_slot(SLOTS, lambda: conf_out(2)), at_slot(SLOTS + 1, lambda: conf_glu(2)), at_slot(SLOTS + 2, share_taps),
                             lambda k: some_taps(4) if k > 6 else None))

            pad = lambda buf, lo, back: buf[:, lo:4, PPAD - back:PPAD - back + TOK]

            def window_sums(n):
                src, dst = (px, pa, pb, pa)[n], (pa, pb, pa, pb)[n]
                steps.inc(TT(pad(dst, n, 0), pad(src, n, 0), pad(src, n, 1 << n), ALU.add))
                steps.wait()

            def pool_means():
                for n in range(4):
                    s = (pa if n % 2 == 0 else pb)[:, n, PPAD:PPAD + TOK]
                    steps.inc(TT(s[:, 0:PPAD], s[:, 0:PPAD], cc("inv_count", n * PPAD, PPAD), ALU.mult))
                    steps.inc(TS(s[:, PPAD:TOK], s[:, PPAD:TOK], 1.0 / WINDOWS[n], None, ALU.mult))
                steps.wait()
                for n in range(4):
                    s = (pa if n % 2 == 0 else pb)[:, n, PPAD:PPAD + TOK]
                    ins = TT(s, s, px[:, n, PPAD:PPAD + TOK], ALU.subtract)
                ins.then_inc(pool_made, 1)

            def gated_out(b):
                g = GM["gated"]
                block_done(g, b)
                if b:
                    dve.wait_ge(operand_src, SRC["gated"] + b)
                for i in range(3):
                    scale_out(ua[:, i], (g.first_block + b) % 2, i, 1)

            def gated_conv(b):
                dve.wait_ge(dve_evac, GM["gated"].first_evac + 3 * b + 3)
                t = steps.inc(TT(cvp[:, :, UPAD:UPAD + TOK], ua[:, 1], ua[:, 2], ALU.mult))
                steps.wait(t)
                ts = []
                if b:
                    dve.wait_ge(operand_ready, gated_group(READY, b - 1) + 1)
                for e in range(2):
                    ts.append(steps.inc(TS(ya[:, e], cvp[:, e, 2:2 + TOK], pc("conv_a_w_2", 12 + 2 * b + e), None, ALU.mult)))
                for tap in (1, 0):
                    for e in range(2):
                        steps.wait(ts[e])
                        ts[e] = steps.inc(STT(ya[:, e], cvp[:, e, tap:tap + TOK], pc("conv_a_w_2", 6 * tap + 2 * b + e), ya[:, e], ALU.mult, ALU.add))
                steps.wait()
                TT(ya[:, :, :], ya[:, :, :], ua[:, 0], ALU.mult).then_inc(operand_src, 1)

            def gated_low(b):
                rest_of(y_hi[:, 10 + 2 * b:12 + 2 * b], y_lo[:, 10 + 2 * b:12 + 2 * b], ya[:, :, :], gated_group(READY, b))

            def final_norm_pair(j):
                if j == 0:
                    dve.wait_ge(operand_ready, READY["in_2"] + 8)
                for e in range(2):
                    ins = STT(x[:, 2 * j + e], x[:, 2 * j + e], pc("final_norm_w", 2 * j + e), rstd[:, 0], ALU.mult, ALU.mult)
                upd.inc(ins)

            def ln_centre():
                dve.wait_ge(ln_mean, 1)
                steps.inc(TS(hbuf[:, 0, 0], ps[:, LN_BANKS[0], 0:TOK], 1.0 / WB, None, ALU.mult))
                steps.wait()
                TT(acc[:, :, :], acc[:, :, :], spread(hbuf[:, 0, 0], 6), ALU.subtract).then_inc(ln_centred, 1)

            def ln_scale():
                dve.wait_ge(ln_std, 1)
                steps.inc(nc.vector.reciprocal(hbuf[:, 0, 1], hbuf[:, 0, 1]))
                steps.wait()
                TT(acc[:, :, :], acc[:, :, :], spread(hbuf[:, 0, 1], 6), ALU.mult).then_inc(ln_scaled, 1)

            def beside_gated(b, k):
                if b == 0:
                    if k == 4:
                        take(GM["pool"], lambda b, i: px[:, 2 * i:2 * i + 2, PPAD:PPAD + TOK], 1)(0, 0, GM["pool"].first_block % 2)
                        take(GM["pool"], lambda b, i: px[:, 2 * i:2 * i + 2, PPAD:PPAD + TOK], 1)(0, 1, GM["pool"].first_block % 2)
                    if k == 5:
                        dve.wait_ge(dve_evac, GM["pool"].end_evac)
                    if 5 <= k < 9:
                        window_sums(k - 5)
                    if k == 9:
                        pool_means()
                    if k > 9:
                        some_taps(4)
                if b and k == 4:
                    gated_out(b - 1)
                if b == 1:
                    if k == 5:
                        gated_conv(0)
                    if k == 6:
                        for j in range(2):
                            rest_of(y_hi[:, 2 * j:2 * j + 2], y_lo[:, 2 * j:2 * j + 2], pa[:, 2 * j:2 * j + 2, PPAD:PPAD + TOK], READY["pool"] + j)
                    if k == 9:
                        gated_low(0)
                    if k > 6:
                        some_taps(4)
                if b == 2:
                    if k < 7:
                        some_taps(3)
                    if k == 7:
                        some_taps(len(todo))
                    if k == 8:
                        ln_centre()
                    if k == 9:
                        gated_conv(1)
                    if k == 12:
                        ln_scale()
                    if k == 15:
                        for j in range(3):
                            rest_of(y_hi[:, 4 + 2 * j:6 + 2 * j], y_lo[:, 4 + 2 * j:6 + 2 * j], lnz[:, 2 * j:2 * j + 2], READY["conf"] + j)

            run_product(dve, GM["gated"], split, nothing, also=beside_gated)

            def y_to_x(name):
                def go(j):
                    if j >= 4:
                        upd.wait(upd.n - 3)
                    for e in range(2):
                        steps.inc(STT(hbuf[:, j % 4, e], yres[:, 2 * j + e], pc(name, 2 * j + e), rstd[:, 0], ALU.mult, ALU.mult))
                    steps.wait()
                    t = x[:, 2 * j:2 * j + 2]
                    upd.inc(TT(t, hbuf[:, j % 4], t, ALU.add))
                return go

            run_product(dve, GM["out_2"], split, nothing,
                        both(at_slot(SLOTS, lambda: gated_out(2)), at_slot(SLOTS, lambda: gated_low(1)), at_slot(SLOTS + 1, lambda: gated_conv(2)), at_slot(SLOTS + 3, lambda: gated_low(2)),
                             by_slot(final_norm_pair, 9, range(8))))
            add_norm = y_to_x("norm_mix_post_2")
            upd.wait()
            inverse_root(5)
            for j in range(5):
                if j < 4:
                    add_norm(j)
                if j:
                    up_2_pair(j - 1)
            conv, zeros = feed_forward(GM["up_2"], GM["down_2"], 1, "conv_ffn_w_2", "conv_ffn_bias_2")
            run_product(dve, GM["up_2"], split, conv, slots=ffn_slots, loops=((steps, 16),),
                        first=both(by_slot(add_norm, SLOTS, range(4, 8)), by_slot(up_2_pair, SLOTS + 1, range(4, 8)),
                                   at_slot(9, zeros), at_slot(15, lambda: inverse_root(6))))
            run_product(dve, GM["down_2"], split, nothing, tail(GM["up_2"], conv, ffn_slots))
            add_norm = y_to_x("norm_ffn_post_2")
            inverse_root(7)
            for j in range(8):
                add_norm(j)

        @block.tensor
        def _(pe):
            def mm(out, lhsT, rhs, start, stop):
                return nc.tensor.matmul(out, lhsT, rhs, start=start, stop=stop, skip_group_check=True)

            evacs = {"act": act_evac, "dve": dve_evac, "x": x_updated}
            order = [(g, b) for g in GM.values() for b in range(g.blocks)]

            def product(g, hi, lo, ready, at=None):
                def one(b, parity):
                    if isinstance(b, int):
                        if g.first_block + b >= 2:
                            past, pb_ = order[g.first_block + b - 2]
                            pe.wait_ge(evacs[past.reader], past.first_evac + past.banks * (pb_ + 1))
                    else:
                        pe.wait_ge(evacs[g.reader], g.first_evac + g.banks * b - g.banks)
                    for c in range(g.chunks):
                        if at:
                            at(b, c)
                        s = c % SLOTS
                        pe.wait_ge(chunk_split, g.first_chunk + g.chunks * b + (c + 1))
                        if isinstance(b, int) and b == 0:
                            last_k = min(g.kt - 1, (8 * c + 7) // g.tiles)
                            pe.wait_ge(operand_ready, ready(last_k))
                        if g.token_major:
                            for tok in range(2):
                                ts = slice(tok * P, (tok + 1) * P)
                                for half in range(2):
                                    out = ps[:, 4 * parity + 2 * tok + half]
                                    cs = slice(half * BANK, (half + 1) * BANK)
                                    mm(out, hi[:, c, ts], w_hi[:, s, cs], c == 0, False)
                                    mm(out, hi[:, c, ts], w_lo[:, s, cs], False, False)
                                for half in range(2):
                                    out = ps[:, 4 * parity + 2 * tok + half]
                                    cs = slice(half * BANK, (half + 1) * BANK)
                                    last = mm(out, lo[:, c, ts], w_hi[:, s, cs], False, c == g.chunks - 1)
                        else:
                            for j in range(8):
                                k, t = divmod(8 * c + j, g.tiles)
                                out = ps[:, 4 * parity + t // 2, (t % 2) * TOK:(t % 2 + 1) * TOK]
                                cs = slice(j * P, (j + 1) * P)
                                mm(out, w_hi[:, s, cs], hi[:, k], k == 0 and t % 2 == 0, False)
                                mm(out, w_hi[:, s, cs], lo[:, k], False, False)
                                last = mm(out, w_lo[:, s, cs], hi[:, k], False, k == g.kt - 1)
                        last.then_inc(chunk_used, 1)

                peeled = min(2, g.blocks)
                for b in range(peeled):
                    one(b, (g.first_block + b) % 2)
                pairs = (g.blocks - peeled) // 2
                if pairs < 2:
                    pairs = 0
                if pairs:
                    with pe.Fori(0, pairs) as m:
                        for d in range(2):
                            one(2 * m + (peeled + d), (g.first_block + peeled + d) % 2)
                for b in range(peeled + 2 * pairs, g.blocks):
                    one(b, (g.first_block + b) % 2)

            def sums(n, by_token=False, weighted=False):
                pe.wait_ge(sums_ready, n + 1)
                bank = SUM_BANK[n]
                for e in range(2):
                    last = mm(ps[:, bank, 0:TOK], ones, sumsq[:, e], e == 0, e == 1)
                if by_token:
                    for half in range(2):
                        for e in range(2):
                            last = mm(ps[:, bank, TOK + half:TOK + half + 1], sumsq[:, e, half * P:(half + 1) * P], ones[:, 0:1], e == 0, e == 1)
                if weighted:
                    for e in range(2):
                        last = mm(ps[:, bank, TOK:2 * TOK], ones, sumsq_w[:, e], e == 0, e == 1)
                last.then_inc(sum_done, 1)

            def beside(n, by_token=False, more=None):
                def at(b, c):
                    if isinstance(b, int):
                        if (b, c) == (0, 12):
                            sums(n, by_token)
                        if (b, c) == (1, 0):
                            pe.wait_ge(std_ready, STD_END[n])
                        if more:
                            more(b, c)
                return at

            halves = lambda stage: (lambda k: READY[stage] + k // 2 + 1)

            def beside_first(b, c):
                if (b, c) == (0, 2):
                    pe.wait_ge(table_loaded, 48)
                    mm(ps[0:HEADS, 4, 0:NREL], relb[0:33, :], onehot[:, :], True, True).then_inc(rel_sum, 1)
                if (b, c) == (0, 11):
                    pe.wait_ge(rel_loaded, 16)
                    for h in range(HEADS):
                        last = mm(ps[:, 4 + h // 2, (h % 2) * TOK:(h % 2 + 1) * TOK], flip[:, :], rel_rev[:, h], True, True)
                        if h % 2:
                            last.then_inc(bias_flipped, 1)
                if (b, c) == (0, 13):
                    pe.wait_ge(consts_loaded, 32)
                    pe.wait_ge(bias_made, 4)
                    sums(0, True)
                if (b, c) == (1, 0):
                    pe.wait_ge(std_ready, STD_END[0])

            product(GM["da_fm"], op_hi, op_lo, halves("in"), beside_first)
            product(GM["da_v"], op_hi, op_lo, halves("in"))

            def logits(item, bank0):
                h, qb = divmod(item, 2)
                nk = P * (qb + 1)
                if item:
                    pe.wait_ge(negmax_done, item)
                for m in range(2):
                    ds = slice(m * 64, (m + 1) * 64)
                    last = mm(ps[:, bank0 + m, 0:nk], proj[ds, 24 + h, qb * P:(qb + 1) * P], proj[ds, 32 + h, 0:nk], True, True)
                last.then_inc(logits_done, 1)

            def turn(item, bank0):
                qb = item % 2
                pe.wait_ge(attn_done, item + 1)
                if item:
                    pe.wait_ge(attn_t_done, item)
                for k in range(qb + 1):
                    last = nc.tensor.transpose(ps[:, bank0 + 2, k * P:(k + 1) * P], attn[:, item % 2, k * P:(k + 1) * P], ident)
                last.then_inc(attn_turned, 1)

            def values(item, bank0):
                h, qb = divmod(item, 2)
                pe.wait_ge(attn_t_done, item + 1)
                if h:
                    pe.wait_ge(da_copied, h)
                for k in range(qb + 1):
                    last = mm(ps[:, bank0 + 3, qb * P:(qb + 1) * P], tokv[:, 0, k, h * P:(h + 1) * P],
                              attn_t[:, item % 2, k * P:(k + 1) * P], k == 0, k == qb)
                last.then_inc(av_done, 1)

            def attention(host, c):
                if c == 0 and host:
                    pe.wait_ge(da_copied, 2 * host)
                if c not in HOST_PE:
                    return
                t, item, bank0 = HOST_PE.index(c), 4 * host, host_banks(HOSTS[host])
                if t == 0:
                    past, b = order[GM[HOSTS[host][0]].first_block + HOSTS[host][1] - 1]
                    pe.wait_ge(evacs[past.reader], past.first_evac + past.banks * (b + 1))
                    if host == 0:
                        pe.wait_ge(dve_evac, GM["da_fm"].end_evac)
                if t >= 3:
                    values(item + t - 3, bank0)
                if 2 <= t < 6:
                    turn(item + t - 2, bank0)
                if t < 4:
                    logits(item + t, bank0)

            product(GM["hg_i"], op_hi, op_lo, halves("in"), lambda b, c: attention(0, c))
            product(GM["hg_fm"], op_hi, op_lo, halves("in"), lambda b, c: attention(1 + b, c))

            def head_means(n, src, bank0):
                for j in range(4):
                    pe.wait_ge(head_sq, 4 * n + j + 1)
                    mm(ps[:, bank0 + j], ones, src[:, 2 * j:2 * j + 2], True, True).then_inc(head_mean, 1)
            head_means(0, da_sq, 4)
            pe.wait_ge(dve_evac, GM["hg_fm"].end_evac)

            pe.wait_ge(kdec_made, 1)
            for h in range(HEADS):
                for c in range(2):
                    last = nc.tensor.transpose(ps[:, h // 2, (h % 2) * TOK + c * P:(h % 2) * TOK + (c + 1) * P], r_e[:, h, c * P:(c + 1) * P], ident)
                if h % 2:
                    last.then_inc(kdec_turned, 1)
            pe.wait_ge(kdec_t_done, 4)
            for level in range(7):
                if level >= 2:
                    pe.wait_ge(level_kept, level - 1)
                if level < 6:
                    pe.wait_ge(level_in, level + 1)
                src = (r_j, r_e)[level % 2]
                for h in range(HEADS):
                    for c in range(2):
                        ts = slice(c * P, (c + 1) * P)
                        n = 2 * h + c
                        a, b = (src[:, h, ts], src[:, h, ts]) if level < 6 else (r_kk[:, h, ts], proj[:, h, ts])
                        last = mm(ps[:, 4 * (level % 2) + n // 4, (n % 4) * P:(n % 4 + 1) * P], a, b, True, True)
                last.then_inc(level_mm, 1)

            def outer(c):
                if c == 0:
                    pe.wait_ge(level_kept, 7)
                if c == 2:
                    pe.wait_ge(state_made, 1)
                rows = slice((c % 2) * CH, (c % 2 + 1) * CH)
                for h in range(HEADS):
                    last = mm(ps[:, 2 * (c % 2) + h // 4, (h % 4) * P:(h % 4 + 1) * P],
                              r_f[rows, h, (c // 2) * P:(c // 2 + 1) * P], tokv[rows, 1, c // 2, h * P:(h + 1) * P], True, True)
                last.then_inc(outer_done, 1)

            def recurrence(j):
                pe.wait_ge(state_made, NCHK - 1)
                for h in (2 * j, 2 * j + 1):
                    o = ps[:, j, (h % 2) * TOK:(h % 2 + 1) * TOK]
                    for p in range(2):
                        mm(o[:, p * P:(p + 1) * P], tokv[:, 1, p, h * P:(h + 1) * P], r_h[:, h, p * P:(p + 1) * P], h % 2 == 0 and p == 0, False)
                        for c in range(2 * p, 2 * p + 2):
                            if c:
                                last = mm(o[:, c * CH:(c + 1) * CH], state[:, c - 1, h], r_d[:, h, c * CH:(c + 1) * CH], False, True)
                last.then_inc(rec_done, 1)

            def beside_out(b, c):
                if b:
                    return
                if c == 0:
                    pe.wait_ge(level_kept, 6)
                if c == 1:
                    for chunk in range(NCHK - 1):
                        outer(chunk)
                if c in (2, 3):
                    recurrence(2 * c - 4)
                    recurrence(2 * c - 3)
                if c == 4:
                    head_means(1, r_j, 0)

            mix = lambda k: READY["mix_a"] + k // 2 + 1
            product(GM["out"], op_hi, op_lo, mix, beside_out)
            product(GM["mem_k"], op_hi, op_lo, halves("mem"), beside(1, True))
            product(GM["mem_v"], op_hi, op_lo, halves("mem"))

            def mlogits(item, bank0):
                h, qb = divmod(item, 2)
                if item:
                    pe.wait_ge(mprobs_done, item)
                for d in range(MHT):
                    last = mm(ps[:, bank0, 0:TOK], mq[:, MHT * h + d, qb * P:(qb + 1) * P], mk[:, MHT * h + d], d == 0, d == MHT - 1)
                last.then_inc(mlogits_done, 1)

            def mturn(item, bank0):
                pe.wait_ge(mnormed, item + 1)
                if item:
                    pe.wait_ge(mp_t_done, item)
                for k in range(2):
                    last = nc.tensor.transpose(ps[:, bank0 + 1, k * P:(k + 1) * P], mp[:, item % 2, k * P:(k + 1) * P], ident)
                last.then_inc(mturned, 1)

            def mvalues(h, bank0):
                pe.wait_ge(mp_t_done, 2 * h + 2)
                for j in range(2):
                    q = 2 * h + j
                    if q >= 2:
                        pe.wait_ge(operand_ready, READY["mem_o"] + q - 1)
                    for e in range(2):
                        vt = MHT * h + 2 * j + e
                        for k in range(2):
                            last = mm(ps[:, bank0 + 2 + j, e * TOK:(e + 1) * TOK], mv[:, k, vt * P:(vt + 1) * P], mp_t[:, h % 2, k], e == 0 and k == 0, k == 1)
                    last.then_inc(mpv_done, 1)

            def memory_attention(turn, t):
                bank0, item = memory_banks(turn), 4 * turn
                if t == 0:
                    past, b = order[GM["mem_q"].first_block + turn]
                    pe.wait_ge(evacs[past.reader], past.first_evac + past.banks * (b + 1))
                    pe.wait_ge(dve_evac, GM["mem_k"].end_evac)
                    pe.wait_ge(act_evac, GM["mem_v"].end_evac)
                if t in (4, 6):
                    mvalues(2 * turn + (t - 4) // 2, bank0)
                if 2 <= t < 6:
                    mturn(item + t - 2, bank0)
                if t < 4:
                    mlogits(item + t, bank0)

            def beside_mem_q(b, c):
                if b == 1 and c in HOST_PE:
                    memory_attention(0, HOST_PE.index(c))

            def beside_mem_o(b, c):
                if (b, c) == (0, 0):
                    pe.wait_ge(operand_ready, READY["mem_o"] + 4)
                if b == 0 and c in MEM_PE:
                    memory_attention(1, MEM_PE.index(c))

            product(GM["mem_q"], op_hi, op_lo, halves("mem_q"), beside(2, more=beside_mem_q))
            product(GM["mem_o"], op_hi, op_lo, halves("mem_o"), beside_mem_o)

            each = lambda stage: (lambda k: READY[stage] + k + 1)
            product(GM["up"], op_hi, op_lo, halves("up"), beside(3))
            product(GM["down"], g_hi, g_lo, each("down"))

            def pool_mix():
                pe.wait_ge(pool_made, 1)
                pe.wait_ge(pool_w_loaded, 16)
                for n in range(4):
                    last = mm(ps[:, 3 + 4 * (n // 2), (n % 2) * TOK:(n % 2 + 1) * TOK], pw[:, n], (pa if n % 2 == 0 else pb)[:, n, PPAD:PPAD + TOK], True, True)
                last.then_inc(pool_mixed, 1)

            def ln_sums(src, bank, done):
                for i in range(6):
                    last = mm(ps[:, bank, 0:TOK], ones, src[:, i], i == 0, i == 5)
                last.then_inc(done, 1)

            def beside_conf(b, c):
                if (b, c) == (1, 4):
                    sums(4, weighted=True)

            def beside_gated(b, c):
                if (b, c) == (1, 1):
                    pool_mix()
                if (b, c) == (2, 6):
                    pe.wait_ge(operand_hi, READY["pool"] + 2)
                    pe.wait_ge(ln_src, 4)
                    pe.wait_ge(shared_added, CONF_TAPS - 1)
                    ln_sums(acc, LN_BANKS[0], ln_mean)
                if (b, c) == (2, 9):
                    pe.wait_ge(ln_sq, 1)
                    ln_sums(lnz, LN_BANKS[1], ln_var)

            def beside_out_2(b, c):
                if (b, c) == (0, 0):
                    pe.wait_ge(ln_scaled, 1)

            product(GM["conf"], op_hi, op_lo, halves("in_2"), beside_conf)
            product(GM["pool"], op_hi, op_lo, halves("in_2"))
            product(GM["gated"], op_hi, op_lo, halves("in_2"), beside_gated)
            def mixed(k):
                if k < 4:
                    return READY["pool"] + k // 2 + 1
                return READY["conf"] + (k - 4) // 2 + 1 if k < 10 else gated_group(READY, (k - 10) // 2) + 1 if k >= 12 else READY["conf"] + 3
            product(GM["out_2"], y_hi, y_lo, mixed, beside_out_2)

            def last_sums(n, turn):
                pe.wait_ge(sums_ready, n + 1)
                bank = SUM_BANK[n]
                for e in range(2):
                    mm(ps[:, bank, 0:TOK], ones, sumsq[:, e], e == 0, False)
                for i in range(4):
                    pe.wait_ge(y_squared, 4 * turn + i + 1)
                    for e in range(2):
                        last = mm(ps[:, bank, 0:TOK], ones, hbuf[:, i, e], False, i == 3 and e == 1)
                last.then_inc(sum_done, 1)

            last_sums(5, 0)
            product(GM["up_2"], op_hi, op_lo, halves("up_2"), beside(6))
            product(GM["down_2"], g_hi, g_lo, each("down_2"))
            last_sums(7, 1)


def _tiles(w):
    k, n = w.shape
    return w.reshape(k // P, P, n).transpose(1, 0, 2).reshape(P, -1, CW).transpose(1, 0, 2)


def _columns(v):
    return v.reshape(-1, P).T


def _feature_major(v):
    return v.T.reshape(-1, P, TOK).transpose(1, 0, 2)


def _buckets():
    import numpy as np
    n = np.arange(TOK)
    large = 16 + (np.log(np.maximum(n, 1).astype(np.float32) / np.float32(16)) / np.float32(np.log(8.0))
                  * np.float32(16)).astype(np.int32)
    return np.where(n < 16, n, np.minimum(large, 31))


def _constants():
    import numpy as np
    con = np.zeros((P, NCON), np.float32)
    put = lambda name, v: con.__setitem__((slice(None), slice(CCOL[name], CCOL[name] + v.shape[-1])), v)
    put("ident", np.eye(P))
    put("ones", np.ones((P, P)))
    s, t = np.arange(P)[:, None], np.arange(P)[None, :]
    levels, half = [], CH // 2
    while half:
        levels.append((s // (2 * half) == t // (2 * half)) & (s % (2 * half) < half) & (t % (2 * half) >= half))
        half //= 2
    levels.append(s == t)
    hg = np.concatenate(levels + [np.broadcast_to(np.arange(TOK) % CH != 0, (P, TOK))], axis=1).astype(np.float32)
    put("inv_count", np.concatenate([np.broadcast_to(1.0 / np.minimum(np.arange(PPAD) + 1, w), (P, PPAD)) for w in WINDOWS], axis=1))
    put("eps", np.broadcast_to(np.array([EPS, LN_EPS]), (P, 2)))
    onehot = np.zeros((33, NREL), np.float32)
    bucket = _buckets()
    for i in range(NREL):
        rel = TOK - 1 - i
        onehot[bucket[rel] if rel >= 0 else 32, i] = BIAS_SCALE
    return con, onehot, hg


def kernel(**inputs):
    import numpy as np
    import concourse.bacc as bacc
    from concourse.bass_utils import run_bass_kernel_spmd as run

    a = {n: np.asarray(v) for n, v in inputs.items()}
    m = DM // 2
    w_in, w_kv, w_2 = a["w_in"][0], a["w_mkv"][0], a["w_in_2"][0]
    part = lambda i: w_in[:, i * m:(i + 1) * m]
    weights = [_tiles(part(i)) for i in (0, 1, 2, 5, 4, 3, 6)]
    blocks = lambda w: [_tiles(w[:, i:i + CW]) for i in range(0, w.shape[1], CW)]

    def halves(w):
        return [_tiles(np.concatenate([w[:, i:i + 512], w[:, FF + i:FF + i + 512]], axis=1)) for i in range(0, FF, 512)]
    weights += blocks(a["w_out"][0]) + blocks(w_kv) + blocks(a["w_mq"][0]) + blocks(a["w_mo"][0])
    weights += halves(a["w_up"][0]) + blocks(a["w_down"][0])
    conf, pool = 3 * WB, 5 * WB
    for i in range(0, WB, 256):
        weights.append(_tiles(np.concatenate([w_2[:, conf + i:conf + i + 256], w_2[:, conf + WB + i:conf + WB + i + 256]], axis=1)))
    weights.append(_tiles(w_2[:, pool:]))
    for i in range(0, WB, 256):
        weights.append(_tiles(np.concatenate([w_2[:, j * WB + i:j * WB + i + 256] for j in range(3)], axis=1)))
    w_out_2 = a["w_out_2"][0]
    weights += blocks(np.concatenate([w_out_2[2 * WB:], w_out_2[WB:2 * WB], w_out_2[:WB]], axis=0))
    weights += halves(a["w_up_2"][0]) + blocks(a["w_down_2"][0])
    con, onehot, hg_con = _constants()
    arrays = {
        "weights": np.concatenate(weights),
        "x": _feature_major(a["x"][0]),
        "mem": _feature_major(a["mem"][0]),
        "params": np.concatenate([_columns(a[n]) for n, _ in PARAMS], axis=1),
        "consts": con,
        "hg_consts": hg_con,
        "lam": np.concatenate([a["lam_q1"], a["lam_k1"], a["lam_q2"], a["lam_k2"]]),
        "rel_bias": np.concatenate([a["rel_bias"], np.full((1, HEADS), NEG, np.float32)]),
        "onehot": onehot,
        "flip": np.eye(P, dtype=np.float32)[::-1],
        "pool_w": a["pool_w_2"][0].transpose(1, 0, 2),
    }
    nc = bacc.Bacc("TRN2", target_bir_lowering=False, num_devices=1)
    feed, A = {}, {}
    for n, v in arrays.items():
        feed[f"in_{n}"] = np.ascontiguousarray(v)
        A[n] = nc.dram_tensor(f"in_{n}", v.shape, mybir.dt.from_np(v.dtype), kind="ExternalInput").ap()
    A["out"] = nc.dram_tensor("out_x", (P, KT, TOK), F32, kind="ExternalOutput").ap()
    build(nc, A)
    r = run(nc, [feed], core_ids=[0])
    got = r.results[0]["out_x"]
    return got.transpose(1, 0, 2).reshape(1, DM, TOK).transpose(0, 2, 1)
```
